# Optimizing a Trainium2 kernel written in Bass

```python
import jax, jax.numpy as jnp
from jax import lax
import numpy as np

D_MODEL = 1024
BATCH = 1
SEQ = 256
DEPTH = 1
DEC_BATCH = 8
DEC_SEQ = 1
PAST_LEN = 256
PAGE_SIZE = 128

POOL_WIDTH = D_MODEL // 2
POOL_WINDOWS = (2, 4, 8, 16)
POOL_GROUPS = len(POOL_WINDOWS)
POOL_GC = POOL_WIDTH // POOL_GROUPS
POOL_STATE = max(POOL_WINDOWS) - 1
ATTN_WIDTH = D_MODEL - POOL_WIDTH
HEAD_DIM = 64
N_HEADS = ATTN_WIDTH // HEAD_DIM
MOBA_BLOCK = 256
MOBA_TOPK = 3
QBLK = 32
ROPE_THETA = 10000.0
MEM_LEN = 256
MEM_HEADS = 4
MEM_HEAD_DIM = D_MODEL // MEM_HEADS
D_FF = 4 * D_MODEL
EPS = 1e-6
NEG = -1e30

kernel_name = "hymba_pool_moba_memxattn_step"

def rmsnorm(x, g):
    xf = x.astype(jnp.float32)
    y = xf * lax.rsqrt(jnp.mean(xf * xf, axis=-1, keepdims=True) + EPS)
    return (y * g.astype(jnp.float32)).astype(x.dtype)

def rope(x, pos):
    half = x.shape[-1] // 2
    inv_freq = ROPE_THETA ** (-jnp.arange(half, dtype=jnp.float32) / half)
    ang = pos.astype(jnp.float32)[:, None] * inv_freq[None, :]
    cos = jnp.cos(ang)[None, :, None, :]
    sin = jnp.sin(ang)[None, :, None, :]
    xf = x.astype(jnp.float32)
    x1, x2 = xf[..., :half], xf[..., half:]
    return jnp.concatenate([x1 * cos - x2 * sin, x2 * cos + x1 * sin], axis=-1).astype(x.dtype)

def pool_mix(u, prev, pos0, w_pool, s_pool):
    B, S, _ = u.shape
    ext = jnp.concatenate([prev, u], axis=1)
    extf = ext.astype(jnp.float32)
    cs = jnp.concatenate([jnp.zeros_like(extf[:, :1]), jnp.cumsum(extf, axis=1)], axis=1)
    pos = pos0 + jnp.arange(S)
    outs = []
    for g, w in enumerate(POOL_WINDOWS):
        sl = slice(g * POOL_GC, (g + 1) * POOL_GC)
        wsum = cs[:, POOL_STATE + 1:, sl] - cs[:, POOL_STATE + 1 - w:POOL_STATE + 1 - w + S, sl]
        cnt = jnp.minimum(w, pos + 1).astype(jnp.float32)[None, :, None]
        outs.append(wsum / cnt - extf[:, POOL_STATE:, sl])
    d = jnp.stack(outs, axis=2)
    mixed = jnp.einsum('bsgc,gcd->bsgd', d, w_pool.astype(jnp.float32)).reshape(B, S, POOL_WIDTH)
    out = (mixed * s_pool.astype(jnp.float32)).astype(u.dtype)
    return out, ext[:, -POOL_STATE:]

def moba_attend(q, k, v, q_pos):
    B, Q, H, D = q.shape
    L = k.shape[1]
    nb = -(-L // MOBA_BLOCK)
    pad = nb * MOBA_BLOCK - L
    kb = jnp.pad(k, ((0, 0), (0, pad), (0, 0), (0, 0))).reshape(B, nb, MOBA_BLOCK, H, D).transpose(0, 3, 1, 2, 4)
    vb = jnp.pad(v, ((0, 0), (0, pad), (0, 0), (0, 0))).reshape(B, nb, MOBA_BLOCK, H, D).transpose(0, 3, 1, 2, 4)
    kmean = jnp.mean(kb.astype(jnp.float32), axis=3)
    ksel = min(MOBA_TOPK, nb)
    J = ksel + 1
    scale = D ** -0.5
    bi = jnp.arange(B)[:, None, None, None]
    hi = jnp.arange(H)[None, :, None, None]
    offs = jnp.arange(MOBA_BLOCK)

    def chunk(args):
        qc, pc = args
        C = qc.shape[1]
        qb = pc // MOBA_BLOCK
        s = jnp.einsum('bchd,bhnd->bhcn', qc.astype(jnp.float32), kmean)
        fully_past = jnp.arange(nb)[None, :] < qb[:, None]
        s = jnp.where(fully_past[None, None], s, NEG)
        _, sel = lax.top_k(s, ksel)
        own = jnp.broadcast_to(qb[None, None, :, None], sel.shape[:3] + (1,))
        idx = jnp.concatenate([sel, own], axis=-1)
        ok_blk = jnp.concatenate([sel < qb[None, None, :, None], jnp.ones_like(own, dtype=bool)], axis=-1)
        kg = kb[bi, hi, idx]
        vg = vb[bi, hi, idx]
        kpos = idx[..., None] * MOBA_BLOCK + offs
        ok = ok_blk[..., None] & (kpos <= pc[None, None, :, None, None])
        logits = jnp.einsum('bchd,bhcjkd->bhcjk', qc, kg).astype(jnp.float32) * scale
        logits = jnp.where(ok, logits, NEG)
        p = jax.nn.softmax(logits.reshape(B, H, C, J * MOBA_BLOCK), axis=-1).reshape(B, H, C, J, MOBA_BLOCK)
        return jnp.einsum('bhcjk,bhcjkd->bchd', p.astype(v.dtype), vg)

    C = min(QBLK, Q)
    nq = -(-Q // C)
    padq = nq * C - Q
    qp = jnp.pad(q, ((0, 0), (0, padq), (0, 0), (0, 0))).reshape(B, nq, C, H, D).transpose(1, 0, 2, 3, 4)
    pp = jnp.pad(q_pos, (0, padq), mode='edge').reshape(nq, C)
    out = lax.map(chunk, (qp, pp))
    return out.transpose(1, 0, 2, 3, 4).reshape(B, nq * C, H, D)[:, :Q]

def mem_kv(mem, g_mem, w_ck, w_cv):
    B = mem.shape[0]
    m = rmsnorm(mem, g_mem)
    mk = (m @ w_ck).reshape(B, MEM_LEN, MEM_HEADS, MEM_HEAD_DIM)
    mv = (m @ w_cv).reshape(B, MEM_LEN, MEM_HEADS, MEM_HEAD_DIM)
    return mk, mv

def cross_attend(h, mk, mv, w_cq, w_co):
    B, S, _ = h.shape
    q = (h @ w_cq).reshape(B, S, MEM_HEADS, MEM_HEAD_DIM)
    logits = jnp.einsum('bshd,bmhd->bhsm', q, mk).astype(jnp.float32) * (MEM_HEAD_DIM ** -0.5)
    p = jax.nn.softmax(logits, axis=-1)
    o = jnp.einsum('bhsm,bmhd->bshd', p.astype(mv.dtype), mv).reshape(B, S, D_MODEL)
    return o @ w_co

def decoder_layer(x, pos0, k_past, v_past, pool_prev, mk, mv,
                  g_mix, w_in, w_pool, s_pool, w_out, g_cross, w_cq, w_co, g_mlp, w_up, w_down):
    B, S, _ = x.shape
    pos = pos0 + jnp.arange(S)
    h = rmsnorm(x, g_mix)
    proj = h @ w_in
    o = POOL_WIDTH
    u = proj[..., :o]
    q = rope(proj[..., o:o + ATTN_WIDTH].reshape(B, S, N_HEADS, HEAD_DIM), pos)
    k = rope(proj[..., o + ATTN_WIDTH:o + 2 * ATTN_WIDTH].reshape(B, S, N_HEADS, HEAD_DIM), pos)
    v = proj[..., o + 2 * ATTN_WIDTH:].reshape(B, S, N_HEADS, HEAD_DIM)
    pool_out, pool_new = pool_mix(u, pool_prev, pos0, w_pool, s_pool)
    k_all = jnp.concatenate([k_past, k], axis=1)
    v_all = jnp.concatenate([v_past, v], axis=1)
    attn = moba_attend(q, k_all, v_all, pos).reshape(B, S, ATTN_WIDTH)
    x = x + jnp.concatenate([pool_out, attn], axis=-1) @ w_out
    x = x + cross_attend(rmsnorm(x, g_cross), mk, mv, w_cq, w_co)
    hm = rmsnorm(x, g_mlp)
    x = x + jnp.square(jax.nn.relu(hm @ w_up)) @ w_down
    return x, k, v, pool_new

def setup_inputs(seed: int = 0) -> dict:
    key = jax.random.key(seed)
    ks = jax.random.split(key, 32)
    f32 = jnp.float32

    def nrm(k, shape, scale=1.0):
        return jax.random.normal(k, shape, f32) * scale

    def gain(k, shape):
        return 1.0 + 0.02 * jax.random.normal(k, shape, f32)

    n_pages = PAST_LEN // PAGE_SIZE
    n_used = DEC_BATCH * n_pages
    n_phys = (n_used * 5) // 4
    perm = jax.random.permutation(ks[0], n_phys)
    page_table = perm[:n_used].reshape(DEC_BATCH, n_pages).astype(jnp.int32)
    d = D_MODEL
    return {
        "x_prompt": nrm(ks[1], (BATCH, SEQ, d)),
        "x_sample": nrm(ks[2], (DEC_BATCH, DEC_SEQ, d)),
        "cache_k": nrm(ks[3], (DEPTH, n_phys, PAGE_SIZE, N_HEADS, HEAD_DIM)),
        "cache_v": nrm(ks[4], (DEPTH, n_phys, PAGE_SIZE, N_HEADS, HEAD_DIM)),
        "cache_mem_k": nrm(ks[5], (DEPTH, DEC_BATCH, MEM_LEN, MEM_HEADS, MEM_HEAD_DIM)),
        "cache_mem_v": nrm(ks[6], (DEPTH, DEC_BATCH, MEM_LEN, MEM_HEADS, MEM_HEAD_DIM)),
        "state_pool": nrm(ks[7], (DEPTH, DEC_BATCH, POOL_STATE, POOL_WIDTH)),
        "page_table": page_table,
        "mem_prompt": nrm(ks[8], (BATCH, MEM_LEN, d)),
        "g_mix": gain(ks[9], (DEPTH, d)),
        "w_in": nrm(ks[10], (DEPTH, d, POOL_WIDTH + 3 * ATTN_WIDTH), d ** -0.5),
        "w_pool": nrm(ks[11], (DEPTH, POOL_GROUPS, POOL_GC, POOL_GC), POOL_GC ** -0.5),
        "s_pool": gain(ks[12], (DEPTH, POOL_WIDTH)),
        "w_out": nrm(ks[13], (DEPTH, d, d), d ** -0.5),
        "g_cross": gain(ks[14], (DEPTH, d)),
        "g_mem": gain(ks[15], (DEPTH, d)),
        "w_cq": nrm(ks[16], (DEPTH, d, d), d ** -0.5),
        "w_ck": nrm(ks[17], (DEPTH, d, d), d ** -0.5),
        "w_cv": nrm(ks[18], (DEPTH, d, d), d ** -0.5),
        "w_co": nrm(ks[19], (DEPTH, d, d), d ** -0.5),
        "g_mlp": gain(ks[20], (DEPTH, d)),
        "w_up": nrm(ks[21], (DEPTH, d, D_FF), d ** -0.5),
        "w_down": nrm(ks[22], (DEPTH, D_FF, d), D_FF ** -0.5),
        "g_final": gain(ks[23], (d,)),
    }

def reference(x_prompt, x_sample, cache_k, cache_v, cache_mem_k, cache_mem_v, state_pool, page_table,
              mem_prompt, g_mix, w_in, w_pool, s_pool, w_out, g_cross, g_mem, w_cq, w_ck, w_cv, w_co,
              g_mlp, w_up, w_down, g_final):
    bp = x_prompt.shape[0]
    bs = x_sample.shape[0]
    past_len = page_table.shape[1] * cache_k.shape[2]
    xp, xs = x_prompt, x_sample
    kp_l, vp_l, poolp_l, mkp_l, mvp_l, ks_l, vs_l, pools_l = [], [], [], [], [], [], [], []
    for l in range(DEPTH):
        lp = (g_mix[l], w_in[l], w_pool[l], s_pool[l], w_out[l], g_cross[l], w_cq[l], w_co[l],
              g_mlp[l], w_up[l], w_down[l])
        mk_p, mv_p = mem_kv(mem_prompt, g_mem[l], w_ck[l], w_cv[l])
        empty = jnp.zeros((bp, 0, N_HEADS, HEAD_DIM), xp.dtype)
        pool0 = jnp.zeros((bp, POOL_STATE, POOL_WIDTH), xp.dtype)
        xp, kp, vp, poolp = decoder_layer(xp, 0, empty, empty, pool0, mk_p, mv_p, *lp)
        past_k = cache_k[l][page_table].reshape(bs, past_len, N_HEADS, HEAD_DIM)
        past_v = cache_v[l][page_table].reshape(bs, past_len, N_HEADS, HEAD_DIM)
        xs, ks, vs, pools = decoder_layer(xs, past_len, past_k, past_v, state_pool[l],
                                          cache_mem_k[l], cache_mem_v[l], *lp)
        kp_l.append(kp); vp_l.append(vp); poolp_l.append(poolp); mkp_l.append(mk_p); mvp_l.append(mv_p)
        ks_l.append(ks); vs_l.append(vs); pools_l.append(pools)
    y_prompt = rmsnorm(xp, g_final)
    y_sample = rmsnorm(xs, g_final)
    return (y_prompt, y_sample, jnp.stack(kp_l), jnp.stack(vp_l), jnp.stack(poolp_l), jnp.stack(mkp_l),
            jnp.stack(mvp_l), jnp.stack(ks_l), jnp.stack(vs_l), jnp.stack(pools_l))


_drawn_inputs = setup_inputs


def setup_inputs(seed=0):
    import zlib

    import numpy as np

    out = dict(_drawn_inputs(seed))
    spreads = {}
    factors = {'g_mix': 2.766,
     's_pool': 5.112,
     'g_cross': 8.0,
     'g_mem': 2.854,
     'g_mlp': 10.261,
     'g_final': 8.419}
    for name, (base, spread) in spreads.items():
        noise = np.random.default_rng([zlib.crc32(name.encode()), seed]).standard_normal(out[name].shape)
        drawn = base * np.exp(spread * noise) if base else spread * noise
        out[name] = __import__('jax').numpy.asarray(drawn.astype(out[name].dtype))
    for name, factor in factors.items():
        out[name] = (out[name] * factor).astype(out[name].dtype)
    return out
```

```python
from contextlib import ExitStack

import numpy as np

import concourse.bass as bass
from concourse import mybir

F32 = mybir.dt.float32
F32R = mybir.dt.float32r
I32 = mybir.dt.int32
ALU = mybir.AluOpType
ACT = mybir.ActivationFunctionType
AX_X = mybir.AxisListType.X

P = 128
D = 1024
KT = D // P
SEQ = 256
DEC = 8
T = SEQ + DEC
MEM = 256
HD = 64
NH = 8
MH = 4
MHD = D // MH
AW = NH * HD
AT = AW // P
PAST = 256
PAGE = 128
NPAGES = PAST // PAGE
WINDOWS = (2, 4, 8, 16)
STATE = max(WINDOWS) - 1
FF = 4 * D
FT = FF // P
EPS = 1e-6
NEG = -1e30
THETA = 10000.0
NKEY = PAST + 1

CK = 2
CN = 512
CF = CN // P
RAW = 3
SPLIT = 4
AHEAD = SPLIT - 1
STAGE = 6
KSLOTS = 4
XSLOTS = 8
SOFTS = 3
SOFT_TS = 5

GROUPS = (
    [("in", 1), ("in", 2), ("in", 3), ("in", 0)]
    + [("ck", 0), ("ck", 1), ("cv", 0), ("cv", 1), ("out", 0), ("out", 1), ("cq", 0), ("cq", 1), ("co", 0), ("co", 1)]
    + [("up", n) for n in range(FF // CN)]
    + [("down", n) for n in range(D // CN)]
)
ROWS = {"down": FF}


def plan_chunks():
    chunks = []
    for g, (w, n) in enumerate(GROUPS):
        tiles = ROWS.get(w, D) // P
        for k in range(0, tiles, CK):
            chunks.append((g, w, n, k, k + CK == tiles))
    return chunks


CHUNKS = plan_chunks()
NC = len(CHUNKS)


def banks_of(g):
    w, n = GROUPS[g]
    if w == "cv":
        return (2 * n, 2 * n + 1)
    upper = (w, n) in (("in", 2), ("out", 0), ("cq", 0), ("co", 1), ("down", 1)) or (w == "up" and n % 2 == 1)
    return (4, 5, 6, 7) if upper else (0, 1, 2, 3)


def last_chunk(w, n):
    return max(c for c, x in enumerate(CHUNKS) if x[1] == w and x[2] == n)


def plan_jobs():
    slots = {c: [] for c in range(-1, NC)}

    def put(c, *names):
        slots[c].extend(names)

    put(1, ("stat", "x"))
    k_end, v_end, u_end = last_chunk("in", 2), last_chunk("in", 3), last_chunk("in", 0)
    put(k_end + 1, ("S", 0), ("S", 1))
    put(k_end + 2, ("cS", 0))
    put(k_end + 3, ("P_T", 0), ("P_T", 1), ("S", 2), ("S", 3))
    put(v_end + 1, ("v_nat", 0), ("v_nat", 1), ("v_nat", 2), ("cP_T", 0), ("m_tile", 0), ("m_tile", 1))
    put(v_end + 2, ("O", 0), ("P_T", 2), ("P_T", 3), ("m_tile", 2), ("m_tile", 3))
    put(v_end + 3, ("S", 4), ("S", 5), ("cO", 0), ("m_tile", 4), ("m_tile", 5))
    put(u_end, ("O", 1), ("cS", 1), ("m_tile", 6), ("m_tile", 7))
    put(u_end + 1, ("P_T", 4), ("P_T", 5), ("cP_T", 1), ("S", 6), ("S", 7), ("c_attn", 0))
    put(u_end + 3, ("O", 2), ("P_T", 6), ("P_T", 7), ("stat", "m"), ("stat_col", "m"))
    put(u_end + 5, ("O", 3), ("cO", 1))
    put(u_end + 6, ("pool", 0), ("pool", 1))
    put(u_end + 7, ("pool", 2), ("pool", 3), ("c_attn", 1))
    put(last_chunk("out", 1) + 2, ("stat", "c"))
    a, b = last_chunk("cq", 0), last_chunk("cq", 1)
    put(a + 1, ("xP_S", 0), ("xP_S", 1), ("xS", 0, 0))
    put(a + 2, ("xS", 0, 1))
    put(a + 3, ("xP_T", 0), ("xP_T", 1))
    put(b, ("xP_O", 0), ("xP_O", 1), ("xP_S", 2), ("xS", 1, 0), ("xS", 1, 1), ("xP_T", 2), ("xP_S", 3), ("xP_O", 2),
        ("xc_T", 0), ("xc_T", 1), ("xP_T", 3), ("xc_O", 0, 0), ("xc_O", 0, 1), ("xP_O", 3),
        ("xc_O", 1, 0), ("xc_attn", 0), ("xc_O", 1, 1), ("xc_attn", 1))
    put(last_chunk("co", 1) + 2, ("stat", "f"))
    put(NC - 1, ("stat", "y"))
    return slots


JOBS = plan_jobs()
ORDER = [j for c in range(-1, NC) for j in JOBS[c]]


def plan_banks():
    jobs, groups, uses, stamp, now = {}, {}, [0] * 8, [-1] * 8, 0
    hold_from, hold_to = ORDER.index(("xS", 0, 0)), ORDER.index(("xS", 1, 1))

    def take(bank):
        nonlocal now
        now += 1
        uses[bank] += 1
        stamp[bank] = now
        return uses[bank] - 1

    for c, (g, w, n, k, last) in enumerate(CHUNKS):
        if k == 0:
            for bank in banks_of(g):
                groups[g, bank] = take(bank)
        for j in JOBS[c]:
            if j[0] == "m_tile":
                continue
            if j[0] == "xS" and j != ("xS", 0, 0):
                jobs[j] = jobs["xS", 0, 0]
                continue
            taken = set(banks_of(g)) if not last else set() if (w, n) == ("cq", 1) or g + 1 == len(GROUPS) else set(banks_of(g + 1))
            if hold_from - 2 <= ORDER.index(j) <= hold_to:
                taken.add(7)
            bank = 7 if j[0] == "xS" else min(set(range(8)) - taken, key=lambda b: stamp[b])
            jobs[j] = (bank, take(bank))
    return jobs, groups


PLACE, GROUP_PLACE = plan_banks()


def turns(kinds):
    return {j: i for i, j in enumerate(j for j in ORDER if j[0] in kinds)}


HI = turns(("O", "c_attn", "pool", "xP_O", "xc_attn"))
SOFT = {j: i for i, j in enumerate(j for j in ORDER if j[0] in ("S", "cS", "xP_S") or j == ("xS", 1, 1))}
SOFT_T = turns(("P_T", "cP_T", "xP_T", "xc_T"))
SOFT_END = {("S", h): ("P_T", h) for h in range(NH)} | {("cS", b): ("cP_T", b) for b in range(2)}
SOFT_END |= {("xP_S", h): ("xP_T", h) for h in range(MH)} | {("xS", 1, 1): ("xc_T", 1)}
SOFT_T_END = {("P_T", h): ("O", h // 2) for h in range(NH)} | {("cP_T", b): ("cO", b) for b in range(2)}
SOFT_T_END |= {("xP_T", h): ("xP_O", h) for h in range(MH)} | {("xc_T", b): ("xc_O", b, 1) for b in range(2)}
SOFT_OF = {t: s for s, t in SOFT_END.items()} | {("xc_T", 0): ("xS", 1, 1)}
OPART = turns(("cO", "xc_O"))
OPART_END = {("cO", b): ("c_attn", b) for b in range(2)} | {("xc_O", b, h): ("xc_attn", b) for b in range(2) for h in range(2)}
KEYS_USED = {("xS", 0, 0): 1, ("xS", 0, 1): 2, ("xS", 1, 0): 3}


def before(turn_of, job, slots):
    n = turn_of[job] - slots
    return None if n < 0 else next(j for j, i in turn_of.items() if i == n)


CHUNK_OF = {j: c for c in JOBS for j in JOBS[c]}


def plan_loads(kinds):
    places, windows, at, when = [], [], {}, {}
    for units, slots in kinds:
        place = {}
        for i, (unit, first, last) in enumerate(units):
            prior = units[i - slots][2] if i >= slots else None
            place[unit] = (i % slots, i // slots, prior)
            free = CHUNK_OF[prior] + 7 if prior else 2
            if unit[0] == "mK" and prior is None:
                free = CHUNK_OF["c_attn", 1] + 7
            windows.append((max(free, CHUNK_OF[first] + 3), free, len(windows), unit))
        places.append(place)
    for latest, free, i, unit in sorted(windows, reverse=True):
        c = latest
        while at.get(c) and c > free:
            c -= 1
        if at.get(c):
            c = min(range(free, latest + 1), key=lambda c: len(at.get(c, ())))
        at.setdefault(c, []).append((i, unit))
    return places, {c: [unit for _, unit in sorted(x)] for c, x in at.items()}


UNITS = [(("m", i), ("m_tile", 4 * i), ("m_tile", 4 * i + 3)) for i in range(2)]
UNITS += [(("V", s), ("cO", 0), ("cO", 0)) for s in range(4)]
UNITS += [(("wpool",), ("pool", 0), ("pool", len(WINDOWS) - 1))]
UNITS += [(("V", s), ("cO", 1), ("cO", 1)) for s in range(4, DEC)]
UNITS += [(("mV", b, h, j), ("xc_O", b, h), ("xc_O", b, h)) for b in range(2) for h in range(2) for j in range(4)]
KUNITS = [(("K", s), ("cS", s // 4), ("cS", s // 4)) for s in range(DEC)]
XUNITS = [(("mK", h, s), ("xS", h, s // 4), ("xS", h, s // 4)) for h in range(2) for s in range(DEC)]
(UNIT_PLACE, KEY_PLACE, XKEY_PLACE), LOADS_AT = plan_loads([(UNITS, STAGE), (KUNITS, KSLOTS), (XUNITS, XSLOTS)])


def landing_counts():
    count = {}
    for place in (UNIT_PLACE, KEY_PLACE, XKEY_PLACE):
        total = {}
        for unit, (slot, _, _) in place.items():
            total[slot] = total.get(slot, 0) + 16 * (NPAGES if unit[0] in ("K", "V") else 1)
            count[unit] = total[slot]
    return count


LANDED = landing_counts()


def host_constants():
    pos = np.concatenate([np.arange(SEQ), np.full(DEC, PAST)]).astype(np.float32)
    half = HD // 2
    inv = (THETA ** (-np.arange(half, dtype=np.float64) / half)).astype(np.float32)
    ang = (inv[:, None] * pos[None, :]).astype(np.float32).astype(np.float64)
    cos = np.tile(np.cos(ang), (P // half, 1))
    sin = np.tile(np.concatenate([-np.sin(ang), np.sin(ang)]), (P // HD, 1))
    tri = np.where(np.arange(P)[None, :] <= np.arange(P)[:, None], 0.0, NEG)
    causal = np.concatenate([tri, np.zeros((P, P)), tri], axis=1)
    h = np.arange(32)
    head_q = (2 * np.arange(AT)[None, :, None] + (np.arange(P) // HD)[:, None, None] == h[None, None, :]).reshape(P, AT * 32)
    head_x = np.tile((np.arange(KT)[:, None] // (MHD // P) == h[None, :]).reshape(1, KT * 32), (P, 1))
    row = np.arange(P) % 32
    diag_q = row[:, None] == np.arange(NH)[None, :]
    diag_x = row[:, None] == np.arange(MH)[None, :]
    rowsel = np.arange(P)[:, None] // 32 == np.arange(4)[None, :]
    own = np.zeros((P, 2, P))
    for b in range(2):
        for j in range(4):
            own[4 * b + j, b, 32 * j:32 * j + 32] = 1.0
    pos1 = np.arange(max(WINDOWS)) + 1
    inv_count = np.tile(np.stack([1.0 / np.minimum(w, pos1) for w in WINDOWS]).reshape(1, -1), (P, 1))
    parts = {
        "cos": cos, "sin": sin, "causal": causal, "head_q": head_q, "head_x": head_x, "diag_q": diag_q,
        "diag_x": diag_x, "rowsel": rowsel, "own": own.reshape(P, -1), "inv_count": inv_count,
        "ident": np.eye(P), "ones": np.ones((P, P)),
        "eps": np.full((P, 1), EPS),
    }
    at, n = {}, 0
    for name, a in parts.items():
        at[name] = (n, a.shape[1])
        n += a.shape[1]
    return np.concatenate([np.asarray(a, np.float32) for a in parts.values()], axis=1), at


CONSTANTS, CONST_AT = host_constants()
CONST_COLS = CONSTANTS.shape[1]


def build(nc, ins, outs):
    with ExitStack() as ctx:
        def sb(name, shape, dt=F32, stack=ctx):
            return stack.enter_context(nc.sbuf_tensor(name, shape, dt))

        def sem(name):
            return ctx.enter_context(nc.semaphore(name))

        raw = sb("raw", [P, RAW, CK, CN])
        w_hi = sb("w_hi", [P, SPLIT, CK, CN], F32R)
        w_lo = sb("w_lo", [P, SPLIT, CK, CN], F32R)
        act_hi = sb("act_hi", [P, KT, T], F32R)
        act_lo = sb("act_lo", [P, KT, T], F32R)
        xT = sb("xT", [P, KT, T])
        gains = sb("gains", [P, 6, KT])
        const = sb("const", [P, CONST_COLS])
        rstd = sb("rstd", [P, 2, T])
        std = sb("std", [P, T])
        ssq = sb("ssq", [P, 2, T])
        sq = sb("sq", [P, 2, T])
        cols = sb("cols", [P, 16])
        early = ctx.enter_context(ExitStack())
        mix_hi = sb("mix_hi", [P, KT, T], F32R, early)
        mix_lo = sb("mix_lo", [P, KT, T], F32R, early)
        stage = sb("stage", [P, STAGE, 2 * CN], F32, early)
        keysT = sb("keysT", [P, KSLOTS, AT, NKEY], F32, early)
        qblock = sb("qblock", [P, AT, DEC, 32], F32, early)
        soft = sb("soft", [P, SOFTS, 2 * MEM], F32, early)
        softT = sb("softT", [P, SOFT_TS, 2 * MEM], F32, early)
        stats = sb("stats", [P, SOFTS, 8], F32, early)
        opart = sb("opart", [P, 2, CN], F32, early)
        pages = sb("pages", [1, DEC * NPAGES], I32, early)
        projections = early.enter_context(ExitStack())
        qT = sb("qT", [P, AT, T], F32, projections)
        kT = sb("kT", [P, AT, T], F32, projections)
        vT = sb("vT", [P, AT, T], F32, projections)
        turned = sb("turned", [P, 2, T], F32, projections)
        swapped = sb("swapped", [P, 2, T], F32, projections)
        rope_a = sb("rope_a", [P, 2, T], F32, projections)
        rope_b = sb("rope_b", [P, T], F32, projections)
        projections.close()
        mkT = sb("mkT", [P, KT, MEM], F32, early)
        mv = sb("mv", [P, 2, D], F32, early)
        mixers = early.enter_context(ExitStack())
        sb("beside_projections", [P, (3 * AT + 7) * T - KT * MEM - 2 * D], F32, mixers)
        v_nat = sb("v_nat", [P, 3, AW], F32, mixers)
        ownp = sb("ownp", [DEC, P], F32, mixers)
        uext = sb("uext", [P, AT, STATE + T], F32, mixers)
        stateT = sb("stateT", [P, AT, DEC, STATE], F32, mixers)
        sum_a = sb("sum_a", [P, AT, STATE + T], F32, mixers)
        sum_b = sb("sum_b", [P, AT, STATE + T], F32, mixers)
        mixers.close()
        q2T = sb("q2T", [P, KT, T], F32, early)
        more_keysT = sb("more_keysT", [P, XSLOTS - KSLOTS, AT, NKEY], F32, early)
        early.close()
        hid_hi = sb("hid_hi", [P, FT, T], F32R)
        hid_lo = sb("hid_lo", [P, FT, T], F32R)
        hid = sb("hid", [P, 2, 2, T])
        yT = sb("yT", [P, KT, T])
        psum = ctx.enter_context(nc.psum_tensor("psum", [P, 8, 512], F32))

        def con(name, rows=P):
            at, n = CONST_AT[name]
            return const[0:rows, at:at + n]

        cos, sin, causal, ones = con("cos"), con("sin"), con("causal"), con("ones")
        ident = con("ident")
        eps = con("eps")
        head_q = con("head_q").rearrange("p (k h) -> p k h", h=32)
        head_x = con("head_x").rearrange("p (k h) -> p k h", h=32)
        inv_count = con("inv_count").rearrange("p (g s) -> p g s", g=len(WINDOWS))

        const_landed, gains_landed, pages_landed = sem("const_landed"), sem("gains_landed"), sem("pages_landed")
        x_landed = [sem(f"x_landed{i}") for i in range(2)]
        state_landed = sem("state_landed")
        raw_landed = [sem(f"raw_landed{i}") for i in range(RAW)]
        stage_landed = [sem(f"stage_landed{i}") for i in range(STAGE)]
        keys_landed = [sem(f"keys_landed{i}") for i in range(KSLOTS)]
        xkeys_landed = [sem(f"xkeys_landed{i}") for i in range(XSLOTS)]
        w_hi_ready, w_lo_ready, w_used = sem("w_hi_ready"), sem("w_lo_ready"), sem("w_used")
        bank_full = [sem(f"bank_full{b}") for b in range(8)]
        bank_free = [sem(f"bank_free{b}") for b in range(8)]
        hi_ready = sem("hi_ready")
        stream_hi = sem("stream_hi")
        stream_lo = sem("stream_lo")
        sq_ready, sq_added = sem("sq_ready"), sem("sq_added")
        rstd_ready, cols_ready = sem("rstd_ready"), sem("cols_ready")
        tables_ready = sem("tables_ready")
        swapped_ready, rope_a_ready, rope_done = sem("swapped_ready"), sem("rope_a_ready"), sem("rope_done")
        masked_ready, max_ready, exp_ready, soft_ready = sem("masked_ready"), sem("max_ready"), sem("exp_ready"), sem("soft_ready")
        qblock_ready, own_key_ready, t_copied, keys_used = sem("qblock_ready"), sem("own_key_ready"), sem("t_copied"), sem("keys_used")
        pad_ready, sums_ready, d_ready = sem("pad_ready"), sem("sums_ready"), sem("d_ready")
        relu_ready, square_ready, hid_hi_ready, hid_lo_ready = sem("relu_ready"), sem("square_ready"), sem("hid_hi_ready"), sem("hid_lo_ready")
        y_gained, y_ready = sem("y_gained"), sem("y_ready")
        k_stored, v_stored, u_stored, mk_stored, mv_stored = (sem(f"{x}_stored") for x in ("k", "v", "u", "mk", "mv"))
        stored = sem("stored")
        dve_step = sem("dve_step")

        def wait_full(eng, job):
            bank, n = PLACE[job]
            eng.wait_ge(bank_full[bank], n + 1)

        def wait_out(eng, job):
            bank, n = PLACE[job]
            eng.wait_ge(bank_free[bank], n + 1)

        def bank_of(job, cols=512, rows=P):
            return psum[0:rows, PLACE[job][0], 0:cols]

        def landed(eng, unit):
            for place, sems in ((UNIT_PLACE, stage_landed), (KEY_PLACE, keys_landed), (XKEY_PLACE, xkeys_landed)):
                if unit in place:
                    eng.wait_ge(sems[place[unit][0]], LANDED[unit])

        def staged(unit):
            return stage[:, UNIT_PLACE[unit][0], :]

        def chunked(unit):
            return staged(unit).rearrange("p (c n) -> p c n", c=2)

        def keys_of(unit):
            slot = (KEY_PLACE.get(unit) or XKEY_PLACE[unit])[0]
            return keysT[:, slot] if slot < KSLOTS else more_keysT[:, slot - KSLOTS]

        def wait_mixers_gone(eng):
            eng.wait_ge(v_stored, 48)
            eng.wait_ge(u_stored, 16)
            wait_out(eng, ("c_attn", 1))
            for g in range(len(WINDOWS)):
                wait_out(eng, ("pool", g))

        def difference(g):
            return (sum_a, sum_b)[g % 2][:, g, STATE:]

        def wait_gemm(eng, g, x):
            bank = banks_of(g)[x]
            eng.wait_ge(bank_full[bank], GROUP_PLACE[g, bank] + 1)

        def wait_gemm_out(eng, g, x):
            bank = banks_of(g)[x]
            eng.wait_ge(bank_free[bank], GROUP_PLACE[g, bank] + 1)

        def memory(k):
            return staged(("m", k // 4))[:, (k % 4) * MEM:(k % 4 + 1) * MEM]

        def wait_used(eng, c):
            g, _, _, _, last = CHUNKS[c]
            if last:
                wait_gemm(eng, g, -1)
            else:
                eng.wait_ge(w_used, sum(not x[4] for x in CHUNKS[:c + 1]))

        def mixed(job, part):
            what, *i = job
            B = bank_of(job)
            if what == "O":
                pick, src = lambda t: t[:, AT + i[0], 0:SEQ], B[:, 0:SEQ]
            elif what == "pool":
                pick, src = lambda t: t[:, i[0], :], B[:, 0:T]
            elif what == "xP_O":
                pick, src = lambda t: t[:, 2 * i[0]:2 * i[0] + 2, 0:SEQ], B.rearrange("p (d n) -> p d n", d=2)
            else:
                k0, n, t0 = AT if what == "c_attn" else 0, AT if what == "c_attn" else KT, SEQ + 4 * i[0]
                pick, src = lambda t: t[:, k0:k0 + n, t0:t0 + 4], B[:, 0:4 * n].rearrange("p (k s) -> p k s", s=4)
            return pick(part), src, pick(mix_hi)

        NORM = {"x": 0, "m": 1, "c": 2, "f": 3, "y": 4}

        w_of = {"in": "w_in", "ck": "w_ck", "cv": "w_cv", "out": "w_out", "cq": "w_cq", "co": "w_co", "up": "w_up", "down": "w_down"}
        group = {(w, n): g for g, (w, n) in enumerate(GROUPS)}
        TOK = [(0, P), (P, P), (SEQ, DEC)]
        STREAM = {"x": 0, "m": KT, "out": 2 * KT, "co": 3 * KT}
        GAIN = {"x": 0, "m": 4, "out": 1, "co": 2}

        block = ctx.enter_context(nc.Block())

        @block.sync
        def _(sp):
            page_of = {}

            def load(unit, place, landed_sems):
                slot, _, prior = place[unit]
                done = landed_sems[slot]
                what, *i = unit
                if prior is None:
                    pass
                elif prior in KEYS_USED:
                    sp.wait_ge(keys_used, KEYS_USED[prior])
                elif prior[0] == "m_tile":
                    sp.wait_ge(stream_lo, STREAM["m"] + prior[1] + 1)
                else:
                    wait_full(sp, prior)
                if what == "m":
                    sp.dma_start(staged(unit), ins["mem"][:, i[0]]).then_inc(done, 16)
                elif what == "wpool":
                    sp.dma_start(staged(unit)[:, 0:AW], ins["w_pool"]).then_inc(done, 16)
                elif what == "K":
                    for c in range(NPAGES):
                        p = page_of[i[0], c]
                        sp.dma_start(keys_of(unit)[:, :, c * PAGE:(c + 1) * PAGE], ins["cache_k"][bass.ds(p, 1), :, :, :].rearrange("a p k t -> p (a k) t")).then_inc(done, 16)
                elif what == "V":
                    for c in range(NPAGES):
                        p = page_of[i[0], c]
                        sp.dma_start(staged(unit)[:, c * AW:(c + 1) * AW], ins["cache_v"][bass.ds(p, 1), :, :].rearrange("a t n -> t (a n)")).then_inc(done, 16)
                elif what == "mK":
                    half, s = i
                    if half == 0 and s == 0:
                        wait_mixers_gone(sp)
                    sp.dma_start(keys_of(unit)[:, :, 0:MEM], ins["mem_k"][s, half]).then_inc(done, 16)
                else:
                    b, half, j = i
                    sp.dma_start(staged(unit), ins["mem_v"][4 * b + j, half]).then_inc(done, 16)

            def load_weights(c):
                g, w, n, k, last = CHUNKS[c]
                if c >= RAW:
                    sp.wait_ge(w_lo_ready, c - RAW + 1)
                sp.dma_start(raw[:, c % RAW], ins[w_of[w]][n, k // CK]).then_inc(raw_landed[c % RAW], 16)

            for h in range(2):
                sp.dma_start(xT[:, h * AT:(h + 1) * AT, :], ins["x"][:, h * AT:(h + 1) * AT, :]).then_inc(x_landed[h], 16)
                if h == 0:
                    sp.dma_start(gains[:, :], ins["gains"]).then_inc(gains_landed, 16)
                load_weights(h)
            sp.dma_start(const[:, :], ins["constants"]).then_inc(const_landed, 16)
            sp.dma_start(pages[:, :], ins["page_table"]).then_inc(pages_landed, 16)
            sp.dma_start(stateT[:, :, :, :], ins["state"]).then_inc(state_landed, 16)
            for c in range(2, NC):
                if c == RAW + 1:
                    sp.wait_ge(pages_landed, 16)
                    for s in range(DEC):
                        for i in range(NPAGES):
                            page_of[s, i] = sp.value_load(pages[0:1, s * NPAGES + i:s * NPAGES + i + 1], min_val=0, max_val=ins["cache_k"].shape[0] - 1)
                for unit in LOADS_AT.get(c, ()):
                    for place, sems in ((UNIT_PLACE, stage_landed), (KEY_PLACE, keys_landed), (XKEY_PLACE, xkeys_landed)):
                        if unit in place:
                            load(unit, place, sems)
                load_weights(c)
            sp.dma_start(outs["pool_sample"][0, :, 0:STATE - 1, :], ins["state_pool"][0, :, 1:STATE, :]).then_inc(stored, 16)
            for h in range(4):
                sp.wait_ge(y_ready, h + 1)
                sp.dma_start(outs["y"][:, 2 * h:2 * h + 2, :], yT[:, 2 * h:2 * h + 2, :]).then_inc(stored, 16)
            for done, n in ((k_stored, 1), (v_stored, 3), (u_stored, 1), (mk_stored, 1), (mv_stored, 2), (stored, 5)):
                sp.wait_ge(done, 16 * n)

        @block.tensor
        def _(pe):
            def begin(job):
                bank, n = PLACE[job]
                if n > 0:
                    pe.wait_ge(bank_free[bank], n)

            def end(job, ins_):
                ins_.then_inc(bank_full[PLACE[job][0]], 1)

            def tile4(out, lhsT, rhs, j, start, stop):
                return pe.matmul(out, lhsT, rhs, start=start, stop=stop, skip_group_check=True, tile_position=(0, 32 * j))

            def run(job):
                what, *i = job
                if what == "m_tile":
                    return
                if job != ("xS", 0, 1) and job != ("xS", 1, 0) and job != ("xS", 1, 1):
                    begin(job)
                B = bank_of(job)
                if what == "stat":
                    m = NORM[i[0]]
                    n = MEM if i[0] == "m" else T
                    pe.wait_ge(sq_added, (KT - 1) * (m + 1))
                    last = pe.matmul(B[:, 0:n], ones, ssq[:, m % 2, 0:n], start=True, stop=True)
                elif what == "stat_col":
                    m = NORM[i[0]]
                    for tt, (t0, n) in enumerate(TOK[:2]):
                        last = pe.matmul(B[0:n, tt:tt + 1], ssq[:, m % 2, t0:t0 + n], ones[:, 0:1], start=True, stop=True)
                elif what == "S":
                    h = i[0]
                    if h == 0:
                        pe.wait_ge(rope_done, 2 * AT)
                    r, f = HD * (h % 2), h // 2
                    q, k = qT[r:r + HD, f, :], kT[r:r + HD, f, :]
                    pe.matmul(B[:, 0:P], q[:, 0:P], k[:, 0:P], start=True, stop=True)
                    last = pe.matmul(B[:, P:3 * P], q[:, P:2 * P], k[:, 0:SEQ], start=True, stop=True)
                elif what == "v_nat":
                    t0, n = TOK[i[0]]
                    for f in range(AT):
                        wait_gemm_out(pe, group["in", 3], f)
                        last = pe.transpose(B[0:n, f * P:(f + 1) * P], vT[:, f, t0:t0 + n], ident)
                elif what == "P_T":
                    pe.wait_ge(soft_ready, SOFT[SOFT_OF[job]] + 1)
                    p = soft[:, SOFT[SOFT_OF[job]] % SOFTS, :]
                    for x in range(3):
                        last = pe.transpose(B[:, x * P:(x + 1) * P], p[:, x * P:(x + 1) * P], ident)
                elif what == "O":
                    for e in range(2):
                        h = 2 * i[0] + e
                        t = SOFT_T["P_T", h]
                        wait_out(pe, ("P_T", h))
                        if h == 0:
                            for tt in range(3):
                                wait_out(pe, ("v_nat", tt))
                        o, pT = B[HD * e:HD * e + HD, :], softT[:, t % SOFT_TS, :]
                        pe.matmul(o[:, 0:SEQ], v_nat[:, 0, h * HD:(h + 1) * HD], pT[:, 0:SEQ], start=True, stop=False, skip_group_check=True)
                        last = pe.matmul(o[:, P:SEQ], v_nat[:, 1, h * HD:(h + 1) * HD], pT[:, SEQ:3 * P], start=False, stop=True, skip_group_check=True)
                elif what == "cS":
                    b = i[0]
                    pe.wait_ge(qblock_ready, 1)
                    pe.wait_ge(own_key_ready, 4 * (b + 1))
                    for f in range(AT):
                        for j in range(4):
                            s = 4 * b + j
                            if f == 0:
                                landed(pe, ("K", s))
                            last = tile4(B[32 * j:32 * j + 32, 0:NKEY], qblock[:, f, s, :], keys_of(("K", s))[:, f, :], j, f == 0, f == AT - 1)
                elif what == "cP_T":
                    b = i[0]
                    pe.wait_ge(soft_ready, SOFT[SOFT_OF[job]] + 1)
                    p = soft[:, SOFT[SOFT_OF[job]] % SOFTS, :]
                    for c in range(2):
                        pe.transpose(B[:, c * P:(c + 1) * P], p[:, c * P:(c + 1) * P], ident)
                    last = pe.matmul(B[0:DEC, PAST:PAST + P], p[:, PAST:PAST + 1].broadcast_to([P, DEC]), ident, start=True, stop=True)
                elif what == "cO":
                    b = i[0]
                    wait_out(pe, ("cP_T", b))
                    pT = softT[:, SOFT_T["cP_T", b] % SOFT_TS, :]
                    pe.matmul(B, ownp[:, :], v_nat[0:DEC, 2, :], start=True, stop=False, skip_group_check=True)
                    for c in range(2):
                        for j in range(4):
                            if c == 0:
                                landed(pe, ("V", 4 * b + j))
                            last = tile4(B[32 * j:32 * j + 32, :], pT[:, c * P + 32 * j:c * P + 32 * j + 32], chunked(("V", 4 * b + j))[:, c, :], j, False, c == 1)
                elif what == "c_attn":
                    b = i[0]
                    wait_out(pe, ("cO", b))
                    for f in range(AT):
                        last = pe.matmul(B[:, 4 * f:4 * f + 4], opart[:, OPART["cO", b] % 2, f * P:(f + 1) * P], con("rowsel"), start=True, stop=True)
                elif what == "pool":
                    g = i[0]
                    landed(pe, ("wpool",))
                    pe.wait_ge(d_ready, g + 1)
                    last = pe.matmul(B[:, 0:T], staged(("wpool",))[:, g * P:(g + 1) * P], difference(g), start=True, stop=True)
                elif what == "xS":
                    half, b = i
                    pe.wait_ge(qblock_ready, 2 + half)
                    for f in range(AT):
                        for j in range(4):
                            s = 4 * b + j
                            if f == 0:
                                landed(pe, ("mK", half, s))
                            first = half == 0 and b == 0 and f == 0
                            last = tile4(B[32 * j:32 * j + 32, b * MEM:(b + 1) * MEM], qblock[:, f, s, :], keys_of(("mK", half, s))[:, f, 0:MEM], j, first, half == 1 and f == AT - 1)
                    if (half, b) != (1, 1):
                        last.then_inc(keys_used, 1)
                        return
                elif what == "xP_S":
                    h = i[0]
                    for f in (2 * (h % 2), 2 * (h % 2) + 1):
                        wait_gemm_out(pe, group["cq", h // 2], f)
                    for qt in range(2):
                        for d in range(2):
                            last = pe.matmul(B[:, qt * MEM:(qt + 1) * MEM], q2T[:, 2 * h + d, qt * P:(qt + 1) * P], mkT[:, 2 * h + d, :], start=d == 0, stop=d == 1)
                elif what == "xP_T":
                    pe.wait_ge(soft_ready, SOFT[SOFT_OF[job]] + 1)
                    p = soft[:, SOFT[SOFT_OF[job]] % SOFTS, :]
                    for c in range(2):
                        for qt in range(2):
                            last = pe.transpose(B[:, c * SEQ + qt * P:c * SEQ + (qt + 1) * P], p[:, qt * MEM + c * P:qt * MEM + (c + 1) * P], ident)
                elif what == "xP_O":
                    h = i[0]
                    wait_out(pe, ("xP_T", h))
                    pT = softT[:, SOFT_T["xP_T", h] % SOFT_TS, :]
                    for d in range(2):
                        for c in range(2):
                            last = pe.matmul(B[:, d * SEQ:(d + 1) * SEQ], mv[:, c, h * MHD + d * P:h * MHD + (d + 1) * P], pT[:, c * SEQ:(c + 1) * SEQ], start=c == 0, stop=c == 1)
                elif what == "xc_T":
                    b = i[0]
                    pe.wait_ge(soft_ready, SOFT[SOFT_OF[job]] + 1)
                    p = soft[:, SOFT[SOFT_OF[job]] % SOFTS, :]
                    for c in range(2):
                        last = pe.transpose(B[:, c * P:(c + 1) * P], p[:, b * MEM + c * P:b * MEM + (c + 1) * P], ident)
                elif what == "xc_O":
                    b, half = i
                    wait_out(pe, ("xc_T", b))
                    pT = softT[:, SOFT_T["xc_T", b] % SOFT_TS, :]
                    for c in range(2):
                        for j in range(4):
                            unit = ("mV", b, half, j)
                            if c == 0:
                                landed(pe, unit)
                            last = tile4(B[32 * j:32 * j + 32, :], pT[:, c * P + 32 * j:c * P + 32 * j + 32], chunked(unit)[:, c, :], j, c == 0, c == 1)
                elif what == "xc_attn":
                    b = i[0]
                    for half in range(2):
                        wait_out(pe, ("xc_O", b, half))
                        for f in range(AT):
                            last = pe.matmul(B[:, 4 * (AT * half + f):4 * (AT * half + f) + 4], opart[:, OPART["xc_O", b, half] % 2, f * P:(f + 1) * P], con("rowsel"), start=True, stop=True)
                end(job, last)

            def wait_moving(c):
                g, w, n, k, last = CHUNKS[c]
                if w in ("in", "ck", "cv"):
                    pe.wait_ge(stream_lo, STREAM["x" if w == "in" else "m"] + k + CK)
                elif w == "out":
                    for f in range(k, k + CK):
                        if f < AT:
                            wait_out(pe, ("pool", f))
                        else:
                            wait_out(pe, ("O", f - AT))
                    wait_out(pe, ("c_attn", 1))
                elif w == "cq":
                    pe.wait_ge(stream_lo, STREAM["out"] + k + CK)
                elif w == "co":
                    for f in range(k, k + CK):
                        wait_out(pe, ("xP_O", f // 2))
                    wait_out(pe, ("xc_attn", 1))
                elif w == "up":
                    pe.wait_ge(stream_lo, STREAM["co"] + k + CK)
                elif w == "down":
                    pe.wait_ge(hid_lo_ready, k + CK)

            for c, (g, w, n, k, last_of_group) in enumerate(CHUNKS):
                slot = c % SPLIT
                hi, lo = w_hi[:, slot], w_lo[:, slot]
                pe.wait_ge(w_lo_ready, c + 1)
                wait_moving(c)
                if w in ("in", "cq", "up", "ck", "cv"):
                    mov_hi, mov_lo = act_hi, act_lo
                elif w == "down":
                    mov_hi, mov_lo = hid_hi, hid_lo
                else:
                    mov_hi, mov_lo = mix_hi, mix_lo
                for x, bank in enumerate(banks_of(g)):
                    if k == 0 and GROUP_PLACE[g, bank] > 0:
                        pe.wait_ge(bank_free[bank], GROUP_PLACE[g, bank])
                    for kk in range(CK):
                        first, end_ = k + kk == 0, last_of_group and kk == CK - 1
                        if w == "cv":
                            out = psum[:, bank, :]
                            th, tl = mov_hi[:, k + kk, x * P:(x + 1) * P], mov_lo[:, k + kk, x * P:(x + 1) * P]
                            passes = ((th, hi[:, kk, :]), (tl, hi[:, kk, :]), (th, lo[:, kk, :]))
                        else:
                            N = MEM if w == "ck" else T
                            out = psum[:, bank, 0:N]
                            wh, wl = hi[:, kk, x * P:(x + 1) * P], lo[:, kk, x * P:(x + 1) * P]
                            passes = ((wh, mov_hi[:, k + kk, 0:N]), (wh, mov_lo[:, k + kk, 0:N]), (wl, mov_hi[:, k + kk, 0:N]))
                        for m, (a, b) in enumerate(passes):
                            mm = pe.matmul(out, a, b, start=first and m == 0, stop=end_ and m == 2)
                    if last_of_group and x < len(banks_of(g)) - 1:
                        mm.then_inc(bank_full[bank], 1)
                mm.then_inc(bank_full[bank] if last_of_group else w_used, 1)
                if c == 0:
                    pe.wait_ge(const_landed, 16)
                for job in JOBS[c]:
                    run(job)

        @block.scalar
        def _(act):
            def copy(out, in_, scale=1.0):
                return nc.scalar.activation(out, in_, ACT.Copy, scale=scale)

            def split_hi(c):
                act.wait_ge(raw_landed[c % RAW], 16 * (c // RAW + 1))
                if c >= SPLIT:
                    wait_used(act, c - SPLIT)
                copy(w_hi[:, c % SPLIT], raw[:, c % RAW]).then_inc(w_hi_ready, 1)

            def square(norm, k, src, n):
                m = NORM[norm]
                before_ = (KT - 1) * m + max(k - 2, 0)
                if before_ > 0:
                    act.wait_ge(sq_added, before_)
                if k == 0 and m >= 2:
                    wait_full(act, ("stat", {2: "x", 3: "m", 4: "c"}[m]))
                dst = ssq[:, m % 2, 0:n] if k == 0 else sq[:, k % 2, 0:n]
                nc.scalar.activation(dst, src, ACT.Square).then_inc(sq_ready, 1)

            def own_keys(b):
                for s in range(4 * b, 4 * b + 4):
                    if b:
                        wait_full(act, ("cS", 0))
                    copy(keys_of(("K", s))[:, :, PAST], kT[:, :, SEQ + s]).then_inc(own_key_ready, 1)

            def take_out(c):
                g, w, n, _, _ = CHUNKS[c]
                for x, bank in enumerate(banks_of(g)):
                    src = psum[:, bank, 0:T]
                    k = AT * n + x
                    if w == "in" and n in (1, 2):
                        i = AT * g + x
                        wait_gemm(act, g, x)
                        if i >= 2:
                            act.wait_ge(rope_done, i - 1)
                        for r in range(0, P, 32):
                            o = r ^ 32
                            last = copy(swapped[r:r + 32, i % 2, :], src[o:o + 32, :], HD ** -0.5 if n == 1 else 1.0)
                        last.then_inc(swapped_ready, 1)
                    elif w == "cv":
                        wait_gemm(act, g, x)
                        act.wait_ge(cols_ready, 1)
                        if n == 0 and x == 0:
                            act.wait_ge(k_stored, 16)
                            wait_full(act, ("v_nat", 2))
                            act.wait_ge(own_key_ready, DEC)
                            wait_full(act, ("S", NH - 1))
                        copy(mv[:, x, n * CN:(n + 1) * CN], psum[:, bank, :], cols[:, 2 + x:3 + x]).then_inc(bank_free[bank], 1)
                    elif w in ("out", "co"):
                        wait_gemm_out(act, g, x)
                        copy(act_hi[:, k, :], xT[:, k, :], gains[:, GAIN[w], k:k + 1]).then_inc(stream_hi, 1)
                        square("c" if w == "out" else "f", k, xT[:, k, :], T)
                    elif w == "up":
                        wait_gemm_out(act, g, x)
                        j = k
                        if j >= 2:
                            act.wait_ge(hid_lo_ready, j - 1)
                        nc.scalar.activation(hid[:, 1, j % 2, :], hid[:, 0, j % 2, :], ACT.Square).then_inc(square_ready, 1)
                        act.wait_ge(square_ready, j + 1)
                        copy(hid_hi[:, j, :], hid[:, 1, j % 2, :]).then_inc(hid_hi_ready, 1)
                    elif w == "down":
                        wait_gemm_out(act, g, x)
                        copy(yT[:, k, :], xT[:, k, :], gains[:, 3, k:k + 1]).then_inc(y_gained, 1)
                        square("y", k, xT[:, k, :], T)
                if w == "cv" and n == 1:
                    for tt in range(2):
                        for nn in range(2):
                            wait_gemm_out(act, group["cv", nn], tt)
                        act.dma_start(outs["mem_v_prompt"][0, 0, tt * P:(tt + 1) * P].rearrange("t h d -> t (h d)"), mv[:, tt, :]).then_inc(mv_stored, 16)
                if w == "in" and n == 2:
                    act.wait_ge(rope_done, 2 * AT)
                    act.dma_start(outs["k"], kT[:, :, :]).then_inc(k_stored, 16)
                    own_keys(0)
                if w == "in" and n == 0:
                    for x in range(4):
                        wait_gemm_out(act, g, x)
                    act.dma_start(outs["u"], uext[:, :, SEQ:STATE + T]).then_inc(u_stored, 16)
                if w == "ck" and n == 1:
                    for x in range(4):
                        wait_gemm_out(act, g, x)
                    act.dma_start(outs["mk"], mkT[:, :, :]).then_inc(mk_stored, 16)

            def run(job):
                what, *i = job
                if what == "m_tile":
                    k = i[0]
                    landed(act, ("m", k // 4))
                    wait_used(act, last_chunk("in", 3) + 1 + k // CK)
                    src = memory(k)
                    square("m", k, src, MEM)
                    copy(act_hi[:, k, 0:MEM], src, gains[:, GAIN["m"], k:k + 1]).then_inc(stream_hi, 1)
                    return
                B = bank_of(job)
                free = bank_free[PLACE[job][0]]
                if what == "stat":
                    m = NORM[i[0]]
                    n = MEM if i[0] == "m" else T
                    wait_full(act, job)
                    if m > 0:
                        act.wait_ge(rstd_ready, m)
                    nc.scalar.activation(std[:, 0:n], B[:, 0:n], ACT.Sqrt, bias=eps, scale=1.0 / D).then_inc(free, 1)
                elif what == "stat_col":
                    wait_full(act, job)
                    nc.scalar.activation(cols[:, 0:2], B[:, 0:2], ACT.Sqrt, bias=eps, scale=1.0 / D).then_inc(free, 1)
                elif what == "v_nat":
                    t0, n = TOK[i[0]]
                    wait_full(act, job)
                    copy(v_nat[0:n, i[0], :], B[0:n, :]).then_inc(free, 1)
                    wait_out(act, job)
                    dst = outs["v_prompt"][0, 0, t0:t0 + n].rearrange("t h d -> t (h d)") if i[0] < 2 else outs["v_sample"].rearrange("l b a h d -> (l b a) (h d)")
                    act.dma_start(dst, v_nat[0:n, i[0], :]).then_inc(v_stored, 16)
                elif job in SOFT:
                    slot = SOFT[job] % SOFTS
                    act.wait_ge(max_ready, SOFT[job] + 1)
                    if what == "S":
                        parts = [(soft[:, slot, 0:P],) * 2, (soft[:, slot, P:3 * P],) * 2]
                    elif what == "cS":
                        parts = [(soft[:, slot, 0:NKEY], B[:, 0:NKEY])]
                    else:
                        parts = [(soft[:, slot, x * MEM:(x + 1) * MEM], B[:, x * MEM:(x + 1) * MEM]) for x in range(2)]
                    for x, (dst, src) in enumerate(parts):
                        last = nc.scalar.activation(dst, src, ACT.Exp, bias=stats[:, slot, x:x + 1], accum_out=stats[:, slot, 2 + x:3 + x])
                    last.then_inc(exp_ready if what == "S" else free, 1)
                elif what in ("P_T", "cP_T", "xP_T", "xc_T"):
                    n = SOFT_T[job]
                    wait_full(act, job)
                    prior = before(SOFT_T, job, SOFT_TS)
                    if prior:
                        wait_full(act, SOFT_T_END[prior])
                    size = {"P_T": 3 * P, "cP_T": 2 * P, "xP_T": 2 * SEQ, "xc_T": 2 * P}[what]
                    copy(softT[:, n % SOFT_TS, 0:size], B[:, 0:size]).then_inc(t_copied if what == "cP_T" else free, 1)
                elif what in ("O", "pool", "xP_O", "c_attn", "xc_attn"):
                    wait_full(act, job)
                    dst, src, _ = mixed(job, mix_hi)
                    copy(dst, src, gains[:, 5, i[0]:i[0] + 1] if what == "pool" else 1.0).then_inc(hi_ready, 1)
                if job == ("cS", 0):
                    own_keys(1)

            act.wait_ge(gains_landed, 16)
            for k in range(KT):
                if k == AT:
                    split_hi(0)
                act.wait_ge(x_landed[k // AT], 16)
                copy(act_hi[:, k, :], xT[:, k, :], gains[:, GAIN["x"], k:k + 1]).then_inc(stream_hi, 1)
                square("x", k, xT[:, k, :], T)
            for c in range(1, AHEAD):
                split_hi(c)
            act.wait_ge(const_landed, 16)
            for c in range(NC):
                if c + AHEAD < NC:
                    split_hi(c + AHEAD)
                if CHUNKS[c][4]:
                    take_out(c)
                for job in JOBS[c]:
                    run(job)

        @block.vector
        def _(dve):
            V = nc.vector
            steps = [0]

            def then(ins_):
                steps[0] += 1
                ins_.then_inc(dve_step, 1)
                dve.wait_ge(dve_step, steps[0])

            def split_lo(c):
                dve.wait_ge(w_hi_ready, c + 1)
                V.tensor_tensor(w_lo[:, c % SPLIT], raw[:, c % RAW], w_hi[:, c % SPLIT].bitcast(F32), ALU.subtract).then_inc(w_lo_ready, 1)

            def less(out, src, scale, high):
                return V.scalar_tensor_tensor(out=out, in0=src, scalar=scale, in1=high.bitcast(F32), op0=ALU.mult, op1=ALU.subtract)

            def low_of_square(j):
                dve.wait_ge(hid_hi_ready, j + 1)
                V.tensor_tensor(hid_lo[:, j, :], hid[:, 1, j % 2, :], hid_hi[:, j, :].bitcast(F32), ALU.subtract).then_inc(hid_lo_ready, 1)

            def make_qblock(src, table):
                return V.tensor_tensor(qblock[:, :, :, :], src[:, :, SEQ:T].unsqueeze(3).broadcast_to([P, AT, DEC, 32]),
                                       table.unsqueeze(2).broadcast_to([P, AT, DEC, 32]), ALU.mult)

            def take_out(c):
                g, w, n, _, _ = CHUNKS[c]
                if w in ("ck", "cq", "up"):
                    dve.wait_ge(rstd_ready, {"ck": 2, "cq": 3, "up": 4}[w])
                if w == "cq" and n == 0:
                    wait_mixers_gone(dve)
                if w == "ck" and n == 0:
                    dve.wait_ge(k_stored, 16)
                    dve.wait_ge(own_key_ready, DEC)
                    wait_full(dve, ("S", NH - 1))
                for x, bank in enumerate(banks_of(g)):
                    src = psum[:, bank, 0:T]
                    k = AT * n + x
                    free = bank_free[bank]
                    if w != "cv":
                        wait_gemm(dve, g, x)
                    if w == "in" and n in (1, 2):
                        i = AT * g + x
                        if i == 0:
                            dve.wait_ge(rstd_ready, 1)
                            V.tensor_tensor(turned[:, 0, :], cos, rstd[:, 0, :], ALU.mult)
                            V.tensor_tensor(turned[:, 1, :], sin, rstd[:, 0, :], ALU.mult).then_inc(tables_ready, 1)
                            dve.wait_ge(tables_ready, 1)
                        dve.wait_ge(swapped_ready, i + 1)
                        if i >= 1:
                            dve.wait_ge(rope_done, i)
                        V.scalar_tensor_tensor(out=rope_a[:, i % 2, :], in0=src, scalar=HD ** -0.5 if n == 1 else 1.0, in1=turned[:, 0, :],
                                               op0=ALU.mult, op1=ALU.mult).then_inc(free, 1)
                        V.tensor_tensor(rope_b[:, :], swapped[:, i % 2, :], turned[:, 1, :], ALU.mult).then_inc(rope_a_ready, 1)
                        wait_gemm_out(dve, g, x)
                        dve.wait_ge(rope_a_ready, i + 1)
                        V.tensor_tensor((qT if n == 1 else kT)[:, x, :], rope_a[:, i % 2, :], rope_b[:, :], ALU.add).then_inc(rope_done, 1)
                    elif w == "in":
                        dst = vT[:, x, :] if n == 3 else uext[:, x, STATE:STATE + T]
                        V.tensor_tensor(dst, src, rstd[:, 0, :], ALU.mult).then_inc(free, 1)
                    elif w == "ck":
                        V.tensor_tensor(mkT[:, k, :], psum[:, bank, 0:MEM], rstd[:, 1, 0:MEM], ALU.mult).then_inc(free, 1)
                    elif w in ("out", "co"):
                        V.tensor_tensor(xT[:, k, :], src, xT[:, k, :], ALU.add).then_inc(free, 1)
                        for low in (k - 1,) * (x > 0) + (k,) * (x == 3):
                            dve.wait_ge(stream_hi, STREAM[w] + low + 1)
                            less(act_lo[:, low, :], xT[:, low, :], gains[:, GAIN[w], low:low + 1], act_hi[:, low, :]).then_inc(stream_lo, 1)
                    elif w == "cq":
                        V.scalar_tensor_tensor(out=q2T[:, k, :], in0=src, scalar=MHD ** -0.5, in1=rstd[:, 0, :], op0=ALU.mult, op1=ALU.mult).then_inc(free, 1)
                    elif w == "up":
                        if k >= 2:
                            dve.wait_ge(square_ready, k - 1)
                        V.scalar_tensor_tensor(out=hid[:, 0, k % 2, :], in0=src, scalar=0.0, in1=rstd[:, 1, :], op0=ALU.max, op1=ALU.mult).then_inc(free, 1)
                        if k >= 1:
                            low_of_square(k - 1)
                        if k == FT - 1:
                            low_of_square(k)
                    elif w == "down":
                        V.tensor_tensor(xT[:, k, :], src, xT[:, k, :], ALU.add).then_inc(free, 1)
                if w == "in" and n == 2:
                    make_qblock(qT, head_q).then_inc(qblock_ready, 1)
                if w == "cq":
                    for x in range(4):
                        wait_gemm_out(dve, g, x)
                    if n == 0:
                        wait_full(dve, ("cS", 1))
                    else:
                        dve.wait_ge(keys_used, KEYS_USED["xS", 0, 1])
                    make_qblock(q2T[:, n * AT:(n + 1) * AT, :], head_x[:, n * AT:(n + 1) * AT, :]).then_inc(qblock_ready, 1)

            def pool_differences():
                dve.wait_ge(state_landed, 16)
                dve.wait_ge(sums_ready, 4)
                W = max(WINDOWS)
                for g, w in enumerate(WINDOWS):
                    d, u = difference(g), uext[:, g, STATE:]
                    V.tensor_tensor(d[:, 0:W], d[:, 0:W], inv_count[:, g, :], ALU.mult)
                    V.scalar_tensor_tensor(out=d[:, W:SEQ], in0=d[:, W:SEQ], scalar=1.0 / w, in1=u[:, W:SEQ],
                                           op0=ALU.mult, op1=ALU.subtract)
                    then(V.tensor_reduce(d[:, SEQ:T], stateT[:, g, :, STATE - (w - 1):STATE], AX_X, ALU.add))
                    then(V.tensor_tensor(d[:, SEQ:T], d[:, SEQ:T], u[:, SEQ:T], ALU.add))
                    V.tensor_tensor(d[:, 0:W], d[:, 0:W], u[:, 0:W], ALU.subtract)
                    V.scalar_tensor_tensor(out=d[:, SEQ:T], in0=d[:, SEQ:T], scalar=1.0 / w, in1=u[:, SEQ:T],
                                           op0=ALU.mult, op1=ALU.subtract).then_inc(d_ready, 1)

            def softmax_open(job):
                what, *i = job
                B, slot = bank_of(job), SOFT[job] % SOFTS
                wait_full(dve, job)
                prior = before(SOFT, job, SOFTS)
                if prior:
                    wait_full(dve, SOFT_END[prior])
                if what == "S":
                    V.tensor_tensor(soft[:, slot, 0:3 * P], B[:, 0:3 * P], causal, ALU.add).then_inc(bank_free[PLACE[job][0]], 1)
                    wait_out(dve, job)
                    V.tensor_reduce(stats[:, slot, 0:1], soft[:, slot, 0:P], AX_X, ALU.max, negate=True)
                    V.tensor_reduce(stats[:, slot, 1:2], soft[:, slot, P:3 * P], AX_X, ALU.max, negate=True).then_inc(max_ready, 1)
                elif what == "cS":
                    V.tensor_reduce(stats[:, slot, 0:1], B[:, 0:NKEY], AX_X, ALU.max, negate=True).then_inc(max_ready, 1)
                else:
                    V.tensor_reduce(stats[:, slot, 0:2], B.rearrange("p (x n) -> p x n", x=2), AX_X, ALU.max, negate=True).then_inc(max_ready, 1)

            def softmax_close(job):
                what, *i = job
                slot = SOFT[job] % SOFTS
                if what == "S":
                    dve.wait_ge(exp_ready, i[0] + 1)
                else:
                    wait_out(dve, job)
                n = 1 if what == "cS" else 2
                then(V.reciprocal(stats[:, slot, 4:4 + n], stats[:, slot, 2:2 + n]))
                parts = {"S": [(0, P), (P, 3 * P)], "cS": [(0, NKEY)]}.get(what, [(0, MEM), (MEM, 2 * MEM)])
                for x, (a, b) in enumerate(parts):
                    last = V.tensor_scalar(soft[:, slot, a:b], soft[:, slot, a:b], stats[:, slot, 4 + x:5 + x], None, ALU.mult)
                last.then_inc(soft_ready, 1)

            def run(job):
                what, *i = job
                if what == "m_tile":
                    k = i[0]
                    dve.wait_ge(stream_hi, STREAM["m"] + k + 1)
                    less(act_lo[:, k, 0:MEM], memory(k), gains[:, GAIN["m"], k:k + 1], act_hi[:, k, 0:MEM]).then_inc(stream_lo, 1)
                    return
                if what == "pool" and i[0] == 0:
                    pool_differences()
                B = bank_of(job)
                free = bank_free[PLACE[job][0]]
                if what == "stat":
                    m = NORM[i[0]]
                    n = MEM if i[0] == "m" else T
                    wait_out(dve, job)
                    V.reciprocal(rstd[:, m % 2, 0:n], std[:, 0:n]).then_inc(rstd_ready, 1)
                elif what == "stat_col":
                    wait_out(dve, job)
                    V.reciprocal(cols[:, 2:4], cols[:, 0:2]).then_inc(cols_ready, 1)
                elif what == "cP_T":
                    b = i[0]
                    dve.wait_ge(t_copied, b + 1)
                    if b:
                        wait_full(dve, ("cO", b - 1))
                    V.tensor_tensor(ownp[:, :], B[0:DEC, PAST:PAST + P], con("own", DEC)[:, b * P:(b + 1) * P], ALU.mult).then_inc(free, 1)
                elif what in ("cO", "xc_O"):
                    wait_full(dve, job)
                    prior = before(OPART, job, 2)
                    if prior:
                        wait_full(dve, OPART_END[prior])
                    diag = con("diag_q") if what == "cO" else con("diag_x")[:, 2 * i[1]:2 * i[1] + 2]
                    heads = diag.shape[1]
                    V.tensor_tensor(opart[:, OPART[job] % 2, :].rearrange("p (h n) -> p h n", h=heads), B.rearrange("p (h n) -> p h n", h=heads),
                                    diag.unsqueeze(2).broadcast_to([P, heads, CN // heads]), ALU.mult).then_inc(free, 1)
                elif what in ("O", "xP_O", "c_attn", "xc_attn", "pool"):
                    dve.wait_ge(hi_ready, HI[job] + 1)
                    dst, src, high = mixed(job, mix_lo)
                    if what == "pool":
                        less(dst, src, gains[:, 5, i[0]:i[0] + 1], high).then_inc(free, 1)
                    else:
                        V.tensor_tensor(dst, src, high.bitcast(F32), ALU.subtract).then_inc(free, 1)
            dve.wait_ge(gains_landed, 16)
            for k in range(KT):
                if k == AT:
                    split_lo(0)
                dve.wait_ge(stream_hi, k + 1)
                less(act_lo[:, k, :], xT[:, k, :], gains[:, GAIN["x"], k:k + 1], act_hi[:, k, :]).then_inc(stream_lo, 1)
            for c in range(1, AHEAD):
                split_lo(c)
            dve.wait_ge(const_landed, 16)
            for c in range(NC):
                if c + AHEAD < NC:
                    split_lo(c + AHEAD)
                if CHUNKS[c][4]:
                    take_out(c)
                opened = []
                for job in JOBS[c]:
                    if job[0] == "xS" and job not in SOFT:
                        continue
                    if job in SOFT:
                        softmax_open(job)
                        opened.append(job)
                        if len(opened) == 2:
                            softmax_close(opened.pop(0))
                        continue
                    while opened:
                        softmax_close(opened.pop(0))
                    run(job)
                while opened:
                    softmax_close(opened.pop(0))
            dve.wait_ge(rstd_ready, 5)
            dve.wait_ge(y_gained, KT)
            for h in range(4):
                V.tensor_tensor(yT[:, 2 * h:2 * h + 2, :], yT[:, 2 * h:2 * h + 2, :], rstd[:, 0, :].unsqueeze(1).broadcast_to([P, 2, T]), ALU.mult).then_inc(y_ready, 1)

        @block.gpsimd
        def _(gp):
            def add_squares(norm):
                m = NORM[norm]
                n = MEM if norm == "m" else T
                for k in range(1, KT):
                    gp.wait_ge(sq_ready, KT * m + k + 1)
                    if k > 1:
                        gp.wait_ge(sq_added, (KT - 1) * m + k - 1)
                    nc.gpsimd.tensor_tensor(ssq[:, m % 2, 0:n], ssq[:, m % 2, 0:n], sq[:, k % 2, 0:n], ALU.add).then_inc(sq_added, 1)

            nc.gpsimd.memset(uext[:, :, 0:STATE], 0.0).then_inc(pad_ready, 1)
            add_squares("x")
            add_squares("m")
            gp.wait_ge(pad_ready, 1)
            for f in range(AT):
                wait_gemm_out(gp, group["in", 0], f)
            end_ = STATE + SEQ
            src, dst = uext, sum_a
            for g, w in enumerate(WINDOWS):
                half = w // 2
                if g:
                    gp.wait_ge(sums_ready, g)
                nc.gpsimd.tensor_tensor(dst[:, g:, w - 1:end_], src[:, g:, w - 1:end_], src[:, g:, w - 1 - half:end_ - half], ALU.add).then_inc(sums_ready, 1)
                src, dst = dst, (sum_b, sum_a)[g % 2]
            add_squares("c")
            add_squares("f")
            add_squares("y")


WEIGHTS = ("w_in", "w_out", "w_cq", "w_ck", "w_cv", "w_co", "w_up", "w_down")
DEVICE_OUTPUTS = {
    "y": (P, KT, T), "k": (P, AT, T), "u": (P, AT, STATE + DEC), "mk": (P, KT, MEM),
    "v_prompt": (1, 1, SEQ, NH, HD), "v_sample": (1, DEC, 1, NH, HD), "mem_v_prompt": (1, 1, MEM, MH, MHD), "pool_sample": (1, DEC, STATE, AW),
}


def features_first(a):
    return a.T.reshape(-1, P, a.shape[0]).transpose(1, 0, 2)


def rows_first(a):
    return a.transpose(2, 1, 0).reshape(a.shape[2], -1)


def lay_out(inputs):
    a = {k: np.asarray(v) for k, v in inputs.items()}
    out = {}
    for w in WEIGHTS:
        rows, columns = a[w].shape[1:]
        out[w] = a[w][0].reshape(rows // (CK * P), CK, P, columns // CN, CN).transpose(3, 0, 2, 1, 4)
    out["x"] = features_first(np.concatenate([a["x_prompt"][0], a["x_sample"][:, 0]]))
    out["mem"] = features_first(a["mem_prompt"][0]).reshape(P, 2, 4 * MEM)
    out["gains"] = np.concatenate([a[g].reshape(-1, P).T for g in ("g_mix", "g_cross", "g_mlp", "g_final", "g_mem", "s_pool", "s_pool")], axis=1)
    out["w_pool"] = a["w_pool"][0].transpose(1, 0, 2).reshape(P, AW)
    out["state"] = a["state_pool"][0].reshape(DEC, STATE, AT, P).transpose(3, 2, 0, 1)
    out["state_pool"] = a["state_pool"]
    pages = a["cache_k"].shape[1]
    out["cache_k"] = a["cache_k"][0].reshape(pages, PAGE, AT, P).transpose(0, 3, 2, 1)
    out["cache_v"] = a["cache_v"][0].reshape(pages, PAGE, AW)
    out["mem_k"] = a["cache_mem_k"][0].reshape(DEC, MEM, 2, AT, P).transpose(0, 2, 4, 3, 1)
    out["mem_v"] = a["cache_mem_v"][0].reshape(DEC, 2, P, 2, CN).transpose(0, 3, 2, 1, 4).reshape(DEC, 2, P, 2 * CN)
    out["page_table"] = a["page_table"].reshape(1, -1)
    out["constants"] = CONSTANTS
    return {f"in_{k}": np.ascontiguousarray(v) for k, v in out.items()}


def kernel(**inputs):
    import concourse.bacc as bacc
    from concourse.bass_utils import run_bass_kernel_spmd

    nc = bacc.Bacc("TRN2", target_bir_lowering=False, num_devices=1)
    arrays = lay_out(inputs)
    ins = {name[3:]: nc.dram_tensor(name, a.shape, mybir.dt.from_np(a.dtype), kind="ExternalInput").ap() for name, a in arrays.items()}
    outs = {name: nc.dram_tensor(f"out_{name}", shape, F32, kind="ExternalOutput").ap() for name, shape in DEVICE_OUTPUTS.items()}
    build(nc, ins, outs)
    got = run_bass_kernel_spmd(nc, [arrays], core_ids=[0]).results[0]
    y, k, u = (rows_first(np.asarray(got[f"out_{name}"])) for name in ("y", "k", "u"))
    mk = rows_first(np.asarray(got["out_mk"]))
    pool_sample = np.concatenate([np.asarray(got["out_pool_sample"])[:, :, :STATE - 1], u[STATE:].reshape(1, DEC, 1, AW)], axis=2)
    return (y[:SEQ].reshape(1, SEQ, D), y[SEQ:].reshape(DEC, 1, D), k[:SEQ].reshape(1, 1, SEQ, NH, HD), got["out_v_prompt"],
            u[:STATE].reshape(1, 1, STATE, AW), mk.reshape(1, 1, MEM, MH, MHD), got["out_mem_v_prompt"],
            k[SEQ:].reshape(1, DEC, 1, NH, HD), got["out_v_sample"], pool_sample)
```

```python
from contextlib import ExitStack

import numpy as np

import concourse.bass as bass
from concourse import mybir

F32 = mybir.dt.float32
F32R = mybir.dt.float32r
I32 = mybir.dt.int32
ALU = mybir.AluOpType
ACT = mybir.ActivationFunctionType
AX_X = mybir.AxisListType.X

P = 128
D = 1024
KT = D // P
SEQ = 256
DEC = 8
T = SEQ + DEC
MEM = 256
HD = 64
NH = 8
MH = 4
MHD = D // MH
AW = NH * HD
AT = AW // P
PAST = 256
PAGE = 128
NPAGES = PAST // PAGE
WINDOWS = (2, 4, 8, 16)
STATE = max(WINDOWS) - 1
FF = 4 * D
FT = FF // P
EPS = 1e-6
NEG = -1e30
THETA = 10000.0
NKEY = PAST + 1

CK = 2
CN = 512
RAW, MORE_RAW = 3, 2
SPLIT, MORE_SPLIT = 4, 2
AHEAD = SPLIT - 1
STAGE = 6
KSLOTS = 4
XSLOTS = 8
SQ_SLOTS = 3
SOFTS = 3
SOFT_TS = 5

GROUPS = (
    [("in", 1), ("in", 2), ("in", 3), ("in", 0)]
    + [("ck", 0), ("ck", 1), ("cv", 0), ("cv", 1), ("out", 0), ("out", 1), ("cq", 0), ("cq", 1), ("co", 0), ("co", 1)]
    + [("up", n) for n in range(FF // CN)]
    + [("down", n) for n in range(D // CN)]
)
ROWS = {"down": FF}


def plan_chunks():
    chunks = []
    for g, (w, n) in enumerate(GROUPS):
        tiles = ROWS.get(w, D) // P
        for k in range(0, tiles, CK):
            chunks.append((g, w, n, k, k + CK == tiles))
    return chunks


CHUNKS = plan_chunks()
NC = len(CHUNKS)


FIRST_MLP = next(c for c, x in enumerate(CHUNKS) if x[1] == "up")


def plan_ring(slots, more):
    ring, last, turns_ = [], [None] * (slots + more), [0] * (slots + more)
    for c in range(NC):
        slot = min(range(slots + more if c >= FIRST_MLP else slots), key=lambda i: -1 if last[i] is None else last[i])
        ring.append((slot, turns_[slot], last[slot]))
        last[slot] = c
        turns_[slot] += 1
    return ring


RAW_RING, SPLIT_RING = plan_ring(RAW, MORE_RAW), plan_ring(SPLIT, MORE_SPLIT)


def plan_splits():
    at, c = {}, 0
    for s in range(AHEAD, NC):
        prior = SPLIT_RING[s][2]
        c = max(c + (len(at.get(c, ())) == 2), 0 if prior is None else prior + 1, s - AHEAD if s < FIRST_MLP + 1 else 0)
        at.setdefault(c, []).append(s)
    return at


SPLITS_AT = plan_splits()


def banks_of(g):
    w, n = GROUPS[g]
    if w == "cv":
        return (2 * n, 2 * n + 1)
    upper = (w, n) in (("in", 2), ("ck", 1), ("out", 0), ("cq", 0), ("co", 1), ("down", 1)) or (w == "up" and n % 2 == 1)
    return (4, 5, 6, 7) if upper else (0, 1, 2, 3)


def last_chunk(w, n):
    return max(c for c, x in enumerate(CHUNKS) if x[1] == w and x[2] == n)


def plan_jobs():
    slots = {c: [] for c in range(-1, NC)}

    def put(c, *names):
        slots[c].extend(names)

    put(2, ("stat", "x"))
    k_end, v_end, u_end = last_chunk("in", 2), last_chunk("in", 3), last_chunk("in", 0)
    put(k_end + 2, ("S", 0), ("S", 1))
    put(k_end + 3, ("cS", 0))
    put(v_end, ("P_T", 0), ("P_T", 1), ("S", 2), ("S", 3))
    put(v_end + 1, ("v_nat", 0), ("v_nat", 1), ("v_nat", 2), ("cP_T", 0), ("m_tile", 0), ("m_tile", 1))
    put(v_end + 2, ("P_T", 2), ("P_T", 3), ("O", 0), ("m_tile", 2), ("m_tile", 3))
    put(v_end + 3, ("S", 4), ("S", 5), ("m_tile", 4), ("m_tile", 5))
    put(u_end, ("cO", 0), ("cS", 1), ("O", 1), ("m_tile", 6), ("m_tile", 7))
    put(u_end + 1, ("P_T", 4), ("P_T", 5), ("c_attn", 0))
    put(u_end + 2, ("cP_T", 1), ("S", 6), ("S", 7))
    put(u_end + 3, ("O", 2), ("stat", "m"), ("stat_col", "m"))
    put(u_end + 4, ("differences",))
    put(u_end + 5, ("P_T", 6), ("P_T", 7))
    put(u_end + 6, ("cO", 1), ("O", 3), ("pool", 0), ("pool", 1))
    put(u_end + 7, ("pool", 2), ("pool", 3), ("c_attn", 1))
    put(last_chunk("out", 1) + 3, ("stat", "c"))
    a, b = last_chunk("cq", 0), last_chunk("cq", 1)
    put(a + 1, ("xP_S", 0), ("xP_S", 1), ("xS", 0, 0))
    put(a + 2, ("xS", 0, 1))
    put(a + 3, ("xP_T", 0), ("xP_T", 1))
    put(b, ("xP_O", 0), ("xP_O", 1), ("xP_S", 2), ("xS", 1, 0), ("xS", 1, 1), ("xP_T", 2), ("xP_S", 3), ("xP_O", 2),
        ("xc_T", 0), ("xc_T", 1), ("xP_T", 3), ("xc_O", 0, 0), ("xc_O", 0, 1), ("xP_O", 3),
        ("xc_O", 1, 0), ("xc_attn", 0), ("xc_O", 1, 1), ("xc_attn", 1))
    put(last_chunk("co", 1) + 3, ("stat", "f"))
    put(NC - 1, ("stat", "y"))
    return slots


JOBS = plan_jobs()
ORDER = [j for c in range(-1, NC) for j in JOBS[c]]


def plan_banks():
    jobs, groups, uses, stamp, now = {}, {}, [0] * 8, [-1] * 8, 0
    hold_from, hold_to = ORDER.index(("xS", 0, 0)), ORDER.index(("xS", 1, 1))

    def take(bank):
        nonlocal now
        now += 1
        uses[bank] += 1
        stamp[bank] = now
        return uses[bank] - 1

    for c, (g, w, n, k, last) in enumerate(CHUNKS):
        if k == 0:
            for bank in banks_of(g):
                groups[g, bank] = take(bank)
        for j in JOBS[c]:
            if j[0] in ("m_tile", "differences"):
                continue
            if j[0] == "xS" and j != ("xS", 0, 0):
                jobs[j] = jobs["xS", 0, 0]
                continue
            taken = set(banks_of(g)) if not last else set() if (w, n) == ("cq", 1) or g + 1 == len(GROUPS) else set(banks_of(g + 1))
            if hold_from - 2 <= ORDER.index(j) <= hold_to:
                taken.add(7)
            bank = 7 if j[0] == "xS" else min(set(range(8)) - taken, key=lambda b: stamp[b])
            jobs[j] = (bank, take(bank))
    return jobs, groups


PLACE, GROUP_PLACE = plan_banks()


def turns(kinds):
    return {j: i for i, j in enumerate(j for j in ORDER if j[0] in kinds)}


HI = turns(("O", "c_attn", "pool", "xP_O", "xc_attn"))
SOFT = {j: i for i, j in enumerate(j for j in ORDER if j[0] in ("S", "cS", "xP_S") or j == ("xS", 1, 1))}
SOFT_T = turns(("P_T", "cP_T", "xP_T", "xc_T"))
SOFT_END = {("S", h): ("P_T", h) for h in range(NH)} | {("cS", b): ("cP_T", b) for b in range(2)}
SOFT_END |= {("xP_S", h): ("xP_T", h) for h in range(MH)} | {("xS", 1, 1): ("xc_T", 1)}
SOFT_T_END = {("P_T", h): ("O", h // 2) for h in range(NH)} | {("cP_T", b): ("cO", b) for b in range(2)}
SOFT_T_END |= {("xP_T", h): ("xP_O", h) for h in range(MH)} | {("xc_T", b): ("xc_O", b, 1) for b in range(2)}
SOFT_OF = {t: s for s, t in SOFT_END.items()} | {("xc_T", 0): ("xS", 1, 1)}
OPART = turns(("cO", "xc_O"))
OPART_END = {("cO", b): ("c_attn", b) for b in range(2)} | {("xc_O", b, h): ("xc_attn", b) for b in range(2) for h in range(2)}
KEYS_USED = {("xS", 0, 0): 1, ("xS", 0, 1): 2, ("xS", 1, 0): 3}


def before(turn_of, job, slots):
    n = turn_of[job] - slots
    return None if n < 0 else next(j for j, i in turn_of.items() if i == n)


CHUNK_OF = {j: c for c in JOBS for j in JOBS[c]}


def plan_loads(kinds):
    places, windows, at = [], [], {}
    for units, slots in kinds:
        place = {}
        for i, (unit, first, last) in enumerate(units):
            prior = units[i - slots][2] if i >= slots else None
            place[unit] = (i % slots, i // slots, prior)
            free = CHUNK_OF[prior] + 7 if prior else 2
            if unit[0] == "mK" and prior is None:
                free = CHUNK_OF["cS", 1] + 7 if i < KSLOTS else CHUNK_OF["c_attn", 1] + 7
            windows.append((max(free, CHUNK_OF[first] + 3), free, (ORDER.index(first), len(windows)), unit))
        places.append(place)
    for latest, free, i, unit in sorted(windows, reverse=True):
        c = latest
        while (at.get(c) or (c % 2 == 0 and c > 24)) and c > free:
            c -= 1
        if at.get(c):
            c = min(range(free, latest + 1), key=lambda c: len(at.get(c, ())))
        at.setdefault(c, []).append((i, unit))
    return places, {c: [unit for _, unit in sorted(x)] for c, x in at.items()}


UNITS = [(("m", i), ("m_tile", 4 * i), ("m_tile", 4 * i + 3)) for i in range(2)]
UNITS += [(("V", s), ("cO", 0), ("cO", 0)) for s in range(4)]
UNITS += [(("wpool",), ("pool", 0), ("pool", len(WINDOWS) - 1))]
UNITS += [(("V", s), ("cO", 1), ("cO", 1)) for s in range(4, DEC)]
MV = [(("mV", b, h, j), ("xc_O", b, h), ("xc_O", b, h)) for b in range(2) for h in range(2) for j in range(4)]
UNITS += MV[:STAGE] + MV[STAGE + XSLOTS:]
KUNITS = [(("K", s), ("cS", s // 4), ("cS", s // 4)) for s in range(DEC)]
XUNITS = [(("mK", h, s), ("xS", h, s // 4), ("xS", h, s // 4)) for h in range(2) for s in range(DEC)]
XUNITS += MV[STAGE:STAGE + XSLOTS]
(UNIT_PLACE, KEY_PLACE, XKEY_PLACE), LOADS_AT = plan_loads([(UNITS, STAGE), (KUNITS, KSLOTS), (XUNITS, XSLOTS)])


def landing_counts():
    count = {}
    for place in (UNIT_PLACE, KEY_PLACE, XKEY_PLACE):
        total = {}
        for unit, (slot, _, _) in place.items():
            total[slot] = total.get(slot, 0) + 16 * (NPAGES if unit[0] in ("K", "V") else 1)
            count[unit] = total[slot]
    return count


LANDED = landing_counts()


def host_constants():
    pos = np.concatenate([np.arange(SEQ), np.full(DEC, PAST)]).astype(np.float32)
    half = HD // 2
    inv = (THETA ** (-np.arange(half, dtype=np.float64) / half)).astype(np.float32)
    ang = (inv[:, None] * pos[None, :]).astype(np.float32).astype(np.float64)
    cos = np.tile(np.cos(ang), (P // half, 1))
    sin = np.tile(np.concatenate([-np.sin(ang), np.sin(ang)]), (P // HD, 1))
    tri = np.where(np.arange(P)[None, :] <= np.arange(P)[:, None], 0.0, NEG)
    causal = np.concatenate([tri, np.zeros((P, P)), tri], axis=1)
    h = np.arange(32)
    head_q = (2 * np.arange(AT)[None, :, None] + (np.arange(P) // HD)[:, None, None] == h[None, None, :]).reshape(P, AT * 32)
    head_x = np.tile((np.arange(KT)[:, None] // (MHD // P) == h[None, :]).reshape(1, KT * 32), (P, 1))
    row = np.arange(P) % 32
    diag_q = row[:, None] == np.arange(NH)[None, :]
    diag_x = row[:, None] == np.arange(MH)[None, :]
    rowsel = np.arange(P)[:, None] // 32 == np.arange(4)[None, :]
    own = np.zeros((P, 2, P))
    for b in range(2):
        for j in range(4):
            own[4 * b + j, b, 32 * j:32 * j + 32] = 1.0
    pos1 = np.arange(max(WINDOWS)) + 1
    inv_count = np.tile(np.stack([1.0 / np.minimum(w, pos1) for w in WINDOWS]).reshape(1, -1), (P, 1))
    parts = {
        "cos": cos, "sin": sin, "ones": np.ones((P, P)), "eps": np.full((P, 1), EPS),
        "causal": causal, "head_q": head_q, "head_x": head_x, "diag_q": diag_q,
        "diag_x": diag_x, "rowsel": rowsel, "own": own.reshape(P, -1), "inv_count": inv_count,
        "ident": np.eye(P),
    }
    at, n = {}, 0
    for name, a in parts.items():
        at[name] = (n, a.shape[1])
        n += a.shape[1]
    return np.concatenate([np.asarray(a, np.float32) for a in parts.values()], axis=1), at


CONSTANTS, CONST_AT = host_constants()
CONST_COLS = CONSTANTS.shape[1]
TABLE_COLS = CONST_AT["causal"][0]


def build(nc, ins, outs):
    with ExitStack() as ctx:
        def sb(name, shape, dt=F32, stack=ctx):
            return stack.enter_context(nc.sbuf_tensor(name, shape, dt))

        def sem(name):
            return ctx.enter_context(nc.semaphore(name))

        raw = sb("raw", [P, RAW, CK, CN])
        w_hi = sb("w_hi", [P, SPLIT, CK, CN], F32R)
        w_lo = sb("w_lo", [P, SPLIT, CK, CN], F32R)
        act_hi = sb("act_hi", [P, KT, T], F32R)
        act_lo = sb("act_lo", [P, KT, T], F32R)
        xT = sb("xT", [P, KT, T])
        gains = sb("gains", [P, 6, KT])
        const = sb("const", [P, CONST_COLS])
        rstd = sb("rstd", [P, 2, T])
        std = sb("std", [P, T])
        ssq = sb("ssq", [P, 2, T])
        sq = sb("sq", [P, SQ_SLOTS, T])
        cols = sb("cols", [P, 6])
        early = ctx.enter_context(ExitStack())
        mix_hi = sb("mix_hi", [P, KT, T], F32R, early)
        mix_lo = sb("mix_lo", [P, KT, T], F32R, early)
        stage = sb("stage", [P, STAGE, 2 * CN], F32, early)
        keysT = sb("keysT", [P, KSLOTS, AT, NKEY], F32, early)
        qblock = sb("qblock", [P, AT, DEC, 32], F32, early)
        soft = sb("soft", [P, SOFTS, 2 * MEM], F32, early)
        softT = sb("softT", [P, SOFT_TS, 2 * MEM], F32, early)
        stats = sb("stats", [P, SOFTS, 8], F32, early)
        opart = sb("opart", [P, 2, CN], F32, early)
        pages = sb("pages", [1, DEC * NPAGES], I32, early)
        projections = early.enter_context(ExitStack())
        qT = sb("qT", [P, AT, T], F32, projections)
        kT = sb("kT", [P, AT, T], F32, projections)
        vT = sb("vT", [P, AT, T], F32, projections)
        turned = sb("turned", [P, 2, T], F32, projections)
        swapped = sb("swapped", [P, 2, T], F32, projections)
        rope_a = sb("rope_a", [P, 2, T], F32, projections)
        rope_b = sb("rope_b", [P, 2, T], F32, projections)
        projections.close()
        mkT = sb("mkT", [P, KT, MEM], F32, early)
        mv = sb("mv", [P, 2, D], F32, early)
        mixers = early.enter_context(ExitStack())
        sb("beside_projections", [P, (3 * AT + 8) * T - KT * MEM - 2 * D], F32, mixers)
        v_nat = sb("v_nat", [P, 3, AW], F32, mixers)
        ownp = sb("ownp", [DEC, P], F32, mixers)
        uext = sb("uext", [P, AT, STATE + T], F32, mixers)
        stateT = sb("stateT", [P, AT, DEC, STATE], F32, mixers)
        sum_a = sb("sum_a", [P, AT, STATE + T], F32, mixers)
        sum_b = sb("sum_b", [P, AT, STATE + T], F32, mixers)
        mixers.close()
        q2T = sb("q2T", [P, KT, T], F32, early)
        more_keysT = sb("more_keysT", [P, XSLOTS - KSLOTS, AT, NKEY], F32, early)
        early.close()
        yT = sb("yT", [P, KT, T])
        hid = sb("hid", [P, 2, 2, T])
        last_sq = sb("last_sq", [P, AT, T])
        raw_more = sb("raw_more", [P, MORE_RAW, CK, CN])
        w_hi_more = sb("w_hi_more", [P, MORE_SPLIT, CK, CN], F32R)
        w_lo_more = sb("w_lo_more", [P, MORE_SPLIT, CK, CN], F32R)
        hid_hi = sb("hid_hi", [P, FT, T], F32R)
        hid_lo = sb("hid_lo", [P, FT, T], F32R)
        psum = ctx.enter_context(nc.psum_tensor("psum", [P, 8, 512], F32))

        def con(name, rows=P):
            at, n = CONST_AT[name]
            return const[0:rows, at:at + n]

        cos, sin, causal, ones = con("cos"), con("sin"), con("causal"), con("ones")
        ident = con("ident")
        eps = con("eps")
        head_q = con("head_q").rearrange("p (k h) -> p k h", h=32)
        head_x = con("head_x").rearrange("p (k h) -> p k h", h=32)
        inv_count = con("inv_count").rearrange("p (g s) -> p g s", g=len(WINDOWS))

        tables_landed, const_landed, gains_landed, pages_landed = sem("tables_landed"), sem("const_landed"), sem("gains_landed"), sem("pages_landed")
        x_landed = [sem(f"x_landed{i}") for i in range(4)]
        state_landed = sem("state_landed")
        raw_landed = [sem(f"raw_landed{i}") for i in range(RAW + MORE_RAW)]
        stage_landed = [sem(f"stage_landed{i}") for i in range(STAGE)]
        keys_landed = [sem(f"keys_landed{i}") for i in range(KSLOTS)]
        xkeys_landed = [sem(f"xkeys_landed{i}") for i in range(XSLOTS)]
        w_hi_ready, w_lo_ready, w_used = sem("w_hi_ready"), sem("w_lo_ready"), sem("w_used")
        bank_full = [sem(f"bank_full{b}") for b in range(8)]
        bank_free = [sem(f"bank_free{b}") for b in range(8)]
        hi_ready = sem("hi_ready")
        stream_hi = sem("stream_hi")
        stream_lo = sem("stream_lo")
        sq_ready, sq_added = sem("sq_ready"), sem("sq_added")
        rstd_ready, cols_ready = sem("rstd_ready"), sem("cols_ready")
        tables_ready = sem("tables_ready")
        swapped_ready, rope_b_ready, rope_done = sem("swapped_ready"), sem("rope_b_ready"), sem("rope_done")
        max_ready, exp_ready, soft_ready = sem("max_ready"), sem("exp_ready"), sem("soft_ready")
        qblock_ready, own_key_ready, t_copied, keys_used = sem("qblock_ready"), sem("own_key_ready"), sem("t_copied"), sem("keys_used")
        pad_ready, sums_ready, d_ready = sem("pad_ready"), sem("sums_ready"), sem("d_ready")
        square_ready, hid_hi_ready, hid_lo_ready = sem("square_ready"), sem("hid_hi_ready"), sem("hid_lo_ready")
        y_gained, y_ready = sem("y_gained"), sem("y_ready")
        k_stored, v_stored, u_stored, mk_stored, mv_stored = (sem(f"{x}_stored") for x in ("k", "v", "u", "mk", "mv"))
        stored = sem("stored")
        dve_step = sem("dve_step")

        def wait_full(eng, job):
            bank, n = PLACE[job]
            eng.wait_ge(bank_full[bank], n + 1)

        def wait_out(eng, job):
            bank, n = PLACE[job]
            eng.wait_ge(bank_free[bank], n + 1)

        def bank_of(job, cols=512, rows=P):
            return psum[0:rows, PLACE[job][0], 0:cols]

        def landed(eng, unit):
            for place, sems in ((UNIT_PLACE, stage_landed), (KEY_PLACE, keys_landed), (XKEY_PLACE, xkeys_landed)):
                if unit in place:
                    eng.wait_ge(sems[place[unit][0]], LANDED[unit])

        def staged(unit):
            if unit in UNIT_PLACE:
                return stage[:, UNIT_PLACE[unit][0], :]
            return keys_of(unit).rearrange("p k n -> p (k n)")[:, 0:2 * CN]

        def chunked(unit):
            return staged(unit).rearrange("p (c n) -> p c n", c=2)

        def keys_of(unit):
            slot = (KEY_PLACE.get(unit) or XKEY_PLACE[unit])[0]
            return keysT[:, slot] if slot < KSLOTS else more_keysT[:, slot - KSLOTS]

        def wait_mixers_gone(eng):
            eng.wait_ge(v_stored, 48)
            eng.wait_ge(u_stored, 16)
            wait_out(eng, ("c_attn", 1))
            for g in range(len(WINDOWS)):
                wait_out(eng, ("pool", g))

        def wait_memory_stored(eng):
            eng.wait_ge(mk_stored, 16)
            eng.wait_ge(mv_stored, 32)

        def difference(g):
            return (sum_a, sum_b)[g % 2][:, g, STATE:]

        def wait_gemm(eng, g, x):
            bank = banks_of(g)[x]
            eng.wait_ge(bank_full[bank], GROUP_PLACE[g, bank] + 1)

        def wait_gemm_out(eng, g, x):
            bank = banks_of(g)[x]
            eng.wait_ge(bank_free[bank], GROUP_PLACE[g, bank] + 1)

        def halfway(c):
            return CHUNKS[c][4] and CHUNKS[c][1:3] not in (("cv", 0), ("cv", 1), ("out", 1), ("co", 1))

        def memory(k):
            return staged(("m", k // 4))[:, (k % 4) * MEM:(k % 4 + 1) * MEM]

        def raw_of(c):
            slot = RAW_RING[c][0]
            return raw[:, slot] if slot < RAW else raw_more[:, slot - RAW]

        def hi_of(c):
            slot = SPLIT_RING[c][0]
            return w_hi[:, slot] if slot < SPLIT else w_hi_more[:, slot - SPLIT]

        def lo_of(c):
            slot = SPLIT_RING[c][0]
            return w_lo[:, slot] if slot < SPLIT else w_lo_more[:, slot - SPLIT]

        def wait_used(eng, c):
            g, _, _, _, last = CHUNKS[c]
            if last:
                wait_gemm(eng, g, -1)
            else:
                eng.wait_ge(w_used, sum(not x[4] for x in CHUNKS[:c + 1]))

        def mixed(job, part):
            what, *i = job
            B = bank_of(job)
            if what == "O":
                pick, src = lambda t: t[:, AT + i[0], 0:SEQ], B[:, 0:SEQ]
            elif what == "pool":
                pick, src = lambda t: t[:, i[0], :], B[:, 0:T]
            elif what == "xP_O":
                pick, src = lambda t: t[:, 2 * i[0]:2 * i[0] + 2, 0:SEQ], B.rearrange("p (d n) -> p d n", d=2)
            else:
                k0, n, t0 = AT if what == "c_attn" else 0, AT if what == "c_attn" else KT, SEQ + 4 * i[0]
                pick, src = lambda t: t[:, k0:k0 + n, t0:t0 + 4], B[:, 0:4 * n].rearrange("p (k s) -> p k s", s=4)
            return pick(part), src, pick(mix_hi)

        NORM = {"x": 0, "m": 1, "c": 2, "f": 3, "y": 4}

        w_of = {"in": "w_in", "ck": "w_ck", "cv": "w_cv", "out": "w_out", "cq": "w_cq", "co": "w_co", "up": "w_up", "down": "w_down"}
        group = {(w, n): g for g, (w, n) in enumerate(GROUPS)}
        TOK = [(0, P), (P, P), (SEQ, DEC)]
        STREAM = {"x": 0, "m": KT, "out": 2 * KT, "co": 3 * KT}
        GAIN = {"x": 0, "m": 4, "out": 1, "co": 2}

        block = ctx.enter_context(nc.Block())

        @block.sync
        def _(sp):
            page_of = {}

            def page(s, i):
                if (s, i) not in page_of:
                    page_of[s, i] = sp.value_load(pages[0:1, s * NPAGES + i:s * NPAGES + i + 1], min_val=0, max_val=ins["cache_k"].shape[0] - 1)
                return page_of[s, i]

            def load(unit, place, landed_sems):
                slot, _, prior = place[unit]
                done = landed_sems[slot]
                what, *i = unit
                if prior is None:
                    pass
                elif prior in KEYS_USED:
                    sp.wait_ge(keys_used, KEYS_USED[prior])
                elif prior[0] == "m_tile":
                    sp.wait_ge(stream_lo, STREAM["m"] + prior[1] + 1)
                else:
                    wait_full(sp, prior)
                if what == "m":
                    sp.dma_start(staged(unit), ins["mem"][:, i[0]]).then_inc(done, 16)
                elif what == "wpool":
                    sp.dma_start(staged(unit)[:, 0:AW], ins["w_pool"]).then_inc(done, 16)
                elif what == "K":
                    for c in range(NPAGES):
                        p = page(i[0], c)
                        sp.dma_start(keys_of(unit)[:, :, c * PAGE:(c + 1) * PAGE], ins["cache_k"][bass.ds(p, 1), :, :, :].rearrange("a p k t -> p (a k) t")).then_inc(done, 16)
                elif what == "V":
                    for c in range(NPAGES):
                        p = page(i[0], c)
                        sp.dma_start(staged(unit)[:, c * AW:(c + 1) * AW], ins["cache_v"][bass.ds(p, 1), :, :].rearrange("a t n -> t (a n)")).then_inc(done, 16)
                elif what == "mK":
                    half, s = i
                    if prior is None and slot >= KSLOTS:
                        wait_mixers_gone(sp)
                    elif prior is None:
                        wait_full(sp, ("cS", 1))
                    sp.dma_start(keys_of(unit)[:, :, 0:MEM], ins["mem_k"][s, half]).then_inc(done, 16)
                else:
                    b, half, j = i
                    sp.dma_start(staged(unit), ins["mem_v"][4 * b + j, half]).then_inc(done, 16)

            def load_weights(c):
                g, w, n, k, last = CHUNKS[c]
                slot, _, prior = RAW_RING[c]
                if prior is not None:
                    sp.wait_ge(w_lo_ready, prior + 1)
                elif slot >= RAW:
                    wait_full(sp, ("xc_O", 1, 1))
                sp.dma_start(raw_of(c), ins[w_of[w]][n, k // CK]).then_inc(raw_landed[slot], 16)

            sp.dma_start(gains[:, :], ins["gains"]).then_inc(gains_landed, 16)
            for i in range(4):
                if i < RAW:
                    load_weights(i)
                sp.dma_start(xT[:, CK * i:CK * (i + 1), :], ins["x"][:, CK * i:CK * (i + 1), :]).then_inc(x_landed[i], 16)
            load_weights(RAW)
            sp.dma_start(pages[:, :], ins["page_table"]).then_inc(pages_landed, 16)
            sp.dma_start(const[:, 0:TABLE_COLS], ins["tables"]).then_inc(tables_landed, 16)
            for c in range(RAW + 1, NC):
                if c == RAW + 3:
                    sp.wait_ge(pages_landed, 16)
                for unit in LOADS_AT.get(c, ()):
                    for place, sems in ((UNIT_PLACE, stage_landed), (KEY_PLACE, keys_landed), (XKEY_PLACE, xkeys_landed)):
                        if unit in place:
                            load(unit, place, sems)
                load_weights(c)
                if c == RAW + 2:
                    sp.dma_start(const[:, TABLE_COLS:], ins["constants"]).then_inc(const_landed, 16)
                if c == last_chunk("in", 3):
                    sp.dma_start(stateT[:, :, :, :], ins["state"]).then_inc(state_landed, 16)
            sp.dma_start(outs["pool_sample"][0, :, 0:STATE - 1, :], ins["state_pool"][0, :, 1:STATE, :]).then_inc(stored, 16)
            for h in range(4):
                sp.wait_ge(y_ready, h + 1)
                sp.dma_start(outs["y"][:, 2 * h:2 * h + 2, :], yT[:, 2 * h:2 * h + 2, :]).then_inc(stored, 16)
            for done, n in ((k_stored, 1), (v_stored, 3), (u_stored, 1), (mk_stored, 1), (mv_stored, 2), (stored, 5)):
                sp.wait_ge(done, 16 * n)

        @block.tensor
        def _(pe):
            def begin(job):
                bank, n = PLACE[job]
                if n > 0:
                    pe.wait_ge(bank_free[bank], n)

            def end(job, instruction):
                instruction.then_inc(bank_full[PLACE[job][0]], 1)

            def tile4(out, lhsT, rhs, j, start, stop):
                return pe.matmul(out, lhsT, rhs, start=start, stop=stop, skip_group_check=True, tile_position=(0, 32 * j))

            def run(job):
                what, *i = job
                if what in ("m_tile", "differences"):
                    return
                if job != ("xS", 0, 1) and job != ("xS", 1, 0) and job != ("xS", 1, 1):
                    begin(job)
                B = bank_of(job)
                if what == "stat":
                    m = NORM[i[0]]
                    n = MEM if i[0] == "m" else T
                    if i[0] == "y":
                        pe.wait_ge(sq_added, (KT - 1) * m + AT - 1)
                        pe.matmul(B[:, 0:n], ones, ssq[:, m % 2, 0:n], start=True, stop=False)
                        for k in range(AT, KT):
                            pe.wait_ge(sq_ready, KT * m + k + 1)
                            last = pe.matmul(B[:, 0:n], ones, last_sq[:, k - AT, :], start=False, stop=k == KT - 1)
                    else:
                        pe.wait_ge(sq_added, (KT - 1) * (m + 1))
                        last = pe.matmul(B[:, 0:n], ones, ssq[:, m % 2, 0:n], start=True, stop=True)
                elif what == "stat_col":
                    m = NORM[i[0]]
                    for tt, (t0, n) in enumerate(TOK[:2]):
                        last = pe.matmul(B[0:n, tt:tt + 1], ssq[:, m % 2, t0:t0 + n], ones[:, 0:1], start=True, stop=True)
                elif what == "S":
                    h = i[0]
                    if h == 0:
                        pe.wait_ge(rope_done, 2 * AT)
                    r, f = HD * (h % 2), h // 2
                    q, k = qT[r:r + HD, f, :], kT[r:r + HD, f, :]
                    pe.matmul(B[:, 0:P], q[:, 0:P], k[:, 0:P], start=True, stop=True)
                    last = pe.matmul(B[:, P:3 * P], q[:, P:2 * P], k[:, 0:SEQ], start=True, stop=True)
                elif what == "v_nat":
                    t0, n = TOK[i[0]]
                    for f in range(AT):
                        wait_gemm_out(pe, group["in", 3], f)
                        last = pe.transpose(B[0:n, f * P:(f + 1) * P], vT[:, f, t0:t0 + n], ident)
                elif what == "P_T":
                    pe.wait_ge(soft_ready, SOFT[SOFT_OF[job]] + 1)
                    p = soft[:, SOFT[SOFT_OF[job]] % SOFTS, :]
                    for x in range(3):
                        last = pe.transpose(B[:, x * P:(x + 1) * P], p[:, x * P:(x + 1) * P], ident)
                elif what == "O":
                    for e in range(2):
                        h = 2 * i[0] + e
                        t = SOFT_T["P_T", h]
                        wait_out(pe, ("P_T", h))
                        if h == 0:
                            for tt in range(3):
                                wait_out(pe, ("v_nat", tt))
                        o, pT = B[HD * e:HD * e + HD, :], softT[:, t % SOFT_TS, :]
                        pe.matmul(o[:, 0:SEQ], v_nat[:, 0, h * HD:(h + 1) * HD], pT[:, 0:SEQ], start=True, stop=False, skip_group_check=True)
                        last = pe.matmul(o[:, P:SEQ], v_nat[:, 1, h * HD:(h + 1) * HD], pT[:, SEQ:3 * P], start=False, stop=True, skip_group_check=True)
                elif what == "cS":
                    b = i[0]
                    pe.wait_ge(qblock_ready, 1)
                    pe.wait_ge(own_key_ready, 4 * (b + 1))
                    for f in range(AT):
                        for j in range(4):
                            s = 4 * b + j
                            if f == 0:
                                landed(pe, ("K", s))
                            last = tile4(B[32 * j:32 * j + 32, 0:NKEY], qblock[:, f, s, :], keys_of(("K", s))[:, f, :], j, f == 0, f == AT - 1)
                elif what == "cP_T":
                    b = i[0]
                    pe.wait_ge(soft_ready, SOFT[SOFT_OF[job]] + 1)
                    p = soft[:, SOFT[SOFT_OF[job]] % SOFTS, :]
                    for c in range(2):
                        pe.transpose(B[:, c * P:(c + 1) * P], p[:, c * P:(c + 1) * P], ident)
                    last = pe.matmul(B[0:DEC, PAST:PAST + P], p[:, PAST:PAST + 1].broadcast_to([P, DEC]), ident, start=True, stop=True)
                elif what == "cO":
                    b = i[0]
                    wait_out(pe, ("cP_T", b))
                    pT = softT[:, SOFT_T["cP_T", b] % SOFT_TS, :]
                    pe.matmul(B, ownp[:, :], v_nat[0:DEC, 2, :], start=True, stop=False, skip_group_check=True)
                    for c in range(2):
                        for j in range(4):
                            if c == 0:
                                landed(pe, ("V", 4 * b + j))
                            last = tile4(B[32 * j:32 * j + 32, :], pT[:, c * P + 32 * j:c * P + 32 * j + 32], chunked(("V", 4 * b + j))[:, c, :], j, False, c == 1)
                elif what == "c_attn":
                    b = i[0]
                    wait_out(pe, ("cO", b))
                    for f in range(AT):
                        last = pe.matmul(B[:, 4 * f:4 * f + 4], opart[:, OPART["cO", b] % 2, f * P:(f + 1) * P], con("rowsel"), start=True, stop=True)
                elif what == "pool":
                    g = i[0]
                    landed(pe, ("wpool",))
                    pe.wait_ge(d_ready, g + 1)
                    last = pe.matmul(B[:, 0:T], staged(("wpool",))[:, g * P:(g + 1) * P], difference(g), start=True, stop=True)
                elif what == "xS":
                    half, b = i
                    pe.wait_ge(qblock_ready, 2 + half)
                    for f in range(AT):
                        for j in range(4):
                            s = 4 * b + j
                            if f == 0:
                                landed(pe, ("mK", half, s))
                            first = half == 0 and b == 0 and f == 0
                            last = tile4(B[32 * j:32 * j + 32, b * MEM:(b + 1) * MEM], qblock[:, f, s, :], keys_of(("mK", half, s))[:, f, 0:MEM], j, first, half == 1 and f == AT - 1)
                    if (half, b) != (1, 1):
                        last.then_inc(keys_used, 1)
                        return
                elif what == "xP_S":
                    h = i[0]
                    for f in (2 * (h % 2), 2 * (h % 2) + 1):
                        wait_gemm_out(pe, group["cq", h // 2], f)
                    for qt in range(2):
                        for d in range(2):
                            last = pe.matmul(B[:, qt * MEM:(qt + 1) * MEM], q2T[:, 2 * h + d, qt * P:(qt + 1) * P], mkT[:, 2 * h + d, :], start=d == 0, stop=d == 1)
                elif what == "xP_T":
                    pe.wait_ge(soft_ready, SOFT[SOFT_OF[job]] + 1)
                    p = soft[:, SOFT[SOFT_OF[job]] % SOFTS, :]
                    for c in range(2):
                        for qt in range(2):
                            last = pe.transpose(B[:, c * SEQ + qt * P:c * SEQ + (qt + 1) * P], p[:, qt * MEM + c * P:qt * MEM + (c + 1) * P], ident)
                elif what == "xP_O":
                    h = i[0]
                    wait_out(pe, ("xP_T", h))
                    pT = softT[:, SOFT_T["xP_T", h] % SOFT_TS, :]
                    for d in range(2):
                        for c in range(2):
                            last = pe.matmul(B[:, d * SEQ:(d + 1) * SEQ], mv[:, c, h * MHD + d * P:h * MHD + (d + 1) * P], pT[:, c * SEQ:(c + 1) * SEQ], start=c == 0, stop=c == 1)
                elif what == "xc_T":
                    b = i[0]
                    pe.wait_ge(soft_ready, SOFT[SOFT_OF[job]] + 1)
                    p = soft[:, SOFT[SOFT_OF[job]] % SOFTS, :]
                    for c in range(2):
                        last = pe.transpose(B[:, c * P:(c + 1) * P], p[:, b * MEM + c * P:b * MEM + (c + 1) * P], ident)
                elif what == "xc_O":
                    b, half = i
                    wait_out(pe, ("xc_T", b))
                    pT = softT[:, SOFT_T["xc_T", b] % SOFT_TS, :]
                    for c in range(2):
                        for j in range(4):
                            unit = ("mV", b, half, j)
                            if c == 0:
                                landed(pe, unit)
                            last = tile4(B[32 * j:32 * j + 32, :], pT[:, c * P + 32 * j:c * P + 32 * j + 32], chunked(unit)[:, c, :], j, c == 0, c == 1)
                elif what == "xc_attn":
                    b = i[0]
                    for half in range(2):
                        wait_out(pe, ("xc_O", b, half))
                        for f in range(AT):
                            last = pe.matmul(B[:, 4 * (AT * half + f):4 * (AT * half + f) + 4], opart[:, OPART["xc_O", b, half] % 2, f * P:(f + 1) * P], con("rowsel"), start=True, stop=True)
                end(job, last)

            def wait_moving(c):
                g, w, n, k, last = CHUNKS[c]
                if w in ("in", "ck", "cv"):
                    pe.wait_ge(stream_lo, STREAM["x" if w == "in" else "m"] + k + CK)
                elif w == "out":
                    for f in range(k, k + CK):
                        if f < AT:
                            wait_out(pe, ("pool", f))
                        else:
                            wait_out(pe, ("O", f - AT))
                    wait_out(pe, ("c_attn", 1))
                elif w == "cq":
                    pe.wait_ge(stream_lo, STREAM["out"] + k + CK)
                elif w == "co":
                    for f in range(k, k + CK):
                        wait_out(pe, ("xP_O", f // 2))
                    wait_out(pe, ("xc_attn", 1))
                elif w == "up":
                    pe.wait_ge(stream_lo, STREAM["co"] + k + CK)
                elif w == "down":
                    pe.wait_ge(hid_lo_ready, k + CK)

            for c, (g, w, n, k, last_of_group) in enumerate(CHUNKS):
                hi, lo = hi_of(c), lo_of(c)
                pe.wait_ge(w_lo_ready, c + 1)
                wait_moving(c)
                if w in ("in", "cq", "up", "ck", "cv"):
                    mov_hi, mov_lo = act_hi, act_lo
                elif w == "down":
                    mov_hi, mov_lo = hid_hi, hid_lo
                else:
                    mov_hi, mov_lo = mix_hi, mix_lo
                for x, bank in enumerate(banks_of(g)):
                    if k == 0 and GROUP_PLACE[g, bank] > 0:
                        pe.wait_ge(bank_free[bank], GROUP_PLACE[g, bank])
                    for kk in range(CK):
                        first, end_ = k + kk == 0, last_of_group and kk == CK - 1
                        if w == "cv":
                            out = psum[:, bank, :]
                            th, tl = mov_hi[:, k + kk, x * P:(x + 1) * P], mov_lo[:, k + kk, x * P:(x + 1) * P]
                            passes = ((th, hi[:, kk, :]), (tl, hi[:, kk, :]), (th, lo[:, kk, :]))
                        else:
                            N = MEM if w == "ck" else T
                            out = psum[:, bank, 0:N]
                            wh, wl = hi[:, kk, x * P:(x + 1) * P], lo[:, kk, x * P:(x + 1) * P]
                            passes = ((wh, mov_hi[:, k + kk, 0:N]), (wh, mov_lo[:, k + kk, 0:N]), (wl, mov_hi[:, k + kk, 0:N]))
                        for m, (a, b) in enumerate(passes):
                            mm = pe.matmul(out, a, b, start=first and m == 0, stop=end_ and m == 2)
                    if last_of_group and x < len(banks_of(g)) - 1:
                        mm.then_inc(bank_full[bank], 1)
                mm.then_inc(bank_full[bank] if last_of_group else w_used, 1)
                if JOBS[c] == [("stat", "x")]:
                    pe.wait_ge(tables_landed, 16)
                if c == last_chunk("in", 2):
                    pe.wait_ge(const_landed, 16)
                for job in JOBS[c]:
                    run(job)

        @block.scalar
        def _(act):
            def copy(out, in_, scale=1.0):
                return nc.scalar.activation(out, in_, ACT.Copy, scale=scale)

            def split_hi(c):
                slot, turn, _ = RAW_RING[c]
                act.wait_ge(raw_landed[slot], 16 * (turn + 1))
                slot, _, prior = SPLIT_RING[c]
                if prior is not None:
                    wait_used(act, prior)
                elif slot >= SPLIT:
                    wait_full(act, ("xc_O", 1, 1))
                copy(hi_of(c), raw_of(c)).then_inc(w_hi_ready, 1)

            def square(norm, k, src, n):
                m = NORM[norm]
                added = (KT - 1) * m + max(k - SQ_SLOTS, 0)
                if added > 0:
                    act.wait_ge(sq_added, added)
                if k == 0 and m >= 2:
                    wait_full(act, ("stat", {2: "x", 3: "m", 4: "c"}[m]))
                dst = ssq[:, m % 2, 0:n] if k == 0 else sq[:, k % SQ_SLOTS, 0:n]
                nc.scalar.activation(dst, src, ACT.Square).then_inc(sq_ready, 1)

            def last_square(k):
                nc.scalar.activation(last_sq[:, k - AT, :], xT[:, k, :], ACT.Square).then_inc(sq_ready, 1)

            def own_keys(b):
                for s in range(4 * b, 4 * b + 4):
                    if b:
                        wait_full(act, ("cS", 0))
                    copy(keys_of(("K", s))[:, :, PAST], kT[:, :, SEQ + s]).then_inc(own_key_ready, 1)

            def take_out(c):
                g, w, n, _, _ = CHUNKS[c]
                if w == "up" and n == 0:
                    wait_memory_stored(act)
                for x, bank in enumerate(banks_of(g)):
                    src = psum[:, bank, 0:T]
                    k = AT * n + x
                    if x == 2 and halfway(c):
                        for s in SPLITS_AT.get(c + 1, ()):
                            split_hi(s)
                    if w == "in" and n in (1, 2):
                        i = AT * g + x
                        wait_gemm(act, g, x)
                        if i >= 2:
                            act.wait_ge(rope_done, i - 1)
                        for r in range(0, P, 32):
                            o = r ^ 32
                            last = copy(swapped[r:r + 32, i % 2, :], src[o:o + 32, :], HD ** -0.5 if n == 1 else 1.0)
                        last.then_inc(swapped_ready, 1)
                    elif w == "cv":
                        wait_gemm(act, g, x)
                        act.wait_ge(cols_ready, 1)
                        if n == 0 and x == 0:
                            act.wait_ge(k_stored, 16)
                            wait_full(act, ("v_nat", 2))
                            act.wait_ge(own_key_ready, DEC)
                            wait_full(act, ("S", NH - 1))
                        copy(mv[:, x, n * CN:(n + 1) * CN], psum[:, bank, :], cols[:, 2 + x:3 + x]).then_inc(bank_free[bank], 1)
                    elif w in ("out", "co"):
                        wait_gemm_out(act, g, x)
                        copy(act_hi[:, k, :], xT[:, k, :], gains[:, GAIN[w], k:k + 1]).then_inc(stream_hi, 1)
                        square("c" if w == "out" else "f", k, xT[:, k, :], T)
                    elif w == "up":
                        wait_gemm_out(act, g, x)
                        j = k
                        if j >= 2:
                            act.wait_ge(hid_lo_ready, j - 1)
                        nc.scalar.activation(hid[:, 1, j % 2, :], hid[:, 0, j % 2, :], ACT.Square).then_inc(square_ready, 1)
                        act.wait_ge(square_ready, j + 1)
                        copy(hid_hi[:, j, :], hid[:, 1, j % 2, :]).then_inc(hid_hi_ready, 1)
                    elif w == "down":
                        wait_gemm_out(act, g, x)
                        if n == 0:
                            copy(yT[:, k, :], xT[:, k, :], gains[:, 3, k:k + 1]).then_inc(y_gained, 1)
                            square("y", k, xT[:, k, :], T)
                        else:
                            last_square(k)
                if w == "cv" and n == 1:
                    for tt in range(2):
                        for nn in range(2):
                            wait_gemm_out(act, group["cv", nn], tt)
                        act.dma_start(outs["mem_v_prompt"][0, 0, tt * P:(tt + 1) * P].rearrange("t h d -> t (h d)"), mv[:, tt, :]).then_inc(mv_stored, 16)
                if w == "down" and n == 1:
                    for k in range(AT, KT):
                        copy(yT[:, k, :], xT[:, k, :], gains[:, 3, k:k + 1]).then_inc(y_gained, 1)
                if w == "in" and n == 2:
                    act.wait_ge(rope_done, 2 * AT)
                    act.dma_start(outs["k"], kT[:, :, :]).then_inc(k_stored, 16)
                    own_keys(0)
                if w == "in" and n == 0:
                    for x in range(4):
                        wait_gemm_out(act, g, x)
                    act.dma_start(outs["u"], uext[:, :, SEQ:STATE + T]).then_inc(u_stored, 16)
                if w == "ck" and n == 1:
                    for x in range(4):
                        wait_gemm_out(act, g, x)
                    act.dma_start(outs["mk"], mkT[:, :, :]).then_inc(mk_stored, 16)

            def run(job):
                what, *i = job
                if what == "m_tile":
                    k = i[0]
                    landed(act, ("m", k // 4))
                    wait_used(act, last_chunk("in", 3) + 1 + k // CK)
                    src = memory(k)
                    square("m", k, src, MEM)
                    copy(act_hi[:, k, 0:MEM], src, gains[:, GAIN["m"], k:k + 1]).then_inc(stream_hi, 1)
                    return
                if what == "differences":
                    return
                B = bank_of(job)
                free = bank_free[PLACE[job][0]]
                if what == "stat":
                    m = NORM[i[0]]
                    n = MEM if i[0] == "m" else T
                    wait_full(act, job)
                    if m > 0:
                        act.wait_ge(rstd_ready, m)
                    nc.scalar.activation(std[:, 0:n], B[:, 0:n], ACT.Sqrt, bias=eps, scale=1.0 / D).then_inc(free, 1)
                elif what == "stat_col":
                    wait_full(act, job)
                    nc.scalar.activation(cols[:, 0:2], B[:, 0:2], ACT.Sqrt, bias=eps, scale=1.0 / D).then_inc(free, 1)
                elif what == "v_nat":
                    t0, n = TOK[i[0]]
                    wait_full(act, job)
                    copy(v_nat[0:n, i[0], :], B[0:n, :]).then_inc(free, 1)
                    wait_out(act, job)
                    dst = outs["v_prompt"][0, 0, t0:t0 + n].rearrange("t h d -> t (h d)") if i[0] < 2 else outs["v_sample"].rearrange("l b a h d -> (l b a) (h d)")
                    act.dma_start(dst, v_nat[0:n, i[0], :]).then_inc(v_stored, 16)
                elif job in SOFT:
                    slot = SOFT[job] % SOFTS
                    act.wait_ge(max_ready, SOFT[job] + 1)
                    if what == "S":
                        parts = [(soft[:, slot, 0:P],) * 2, (soft[:, slot, P:3 * P],) * 2]
                    elif what == "cS":
                        parts = [(soft[:, slot, 0:NKEY], B[:, 0:NKEY])]
                    else:
                        parts = [(soft[:, slot, x * MEM:(x + 1) * MEM], B[:, x * MEM:(x + 1) * MEM]) for x in range(2)]
                    for x, (dst, src) in enumerate(parts):
                        last = nc.scalar.activation(dst, src, ACT.Exp, bias=stats[:, slot, x:x + 1], accum_out=stats[:, slot, 2 + x:3 + x])
                    last.then_inc(exp_ready if what == "S" else free, 1)
                elif what in ("P_T", "cP_T", "xP_T", "xc_T"):
                    n = SOFT_T[job]
                    wait_full(act, job)
                    prior = before(SOFT_T, job, SOFT_TS)
                    if prior:
                        wait_full(act, SOFT_T_END[prior])
                    size = {"P_T": 3 * P, "cP_T": 2 * P, "xP_T": 2 * SEQ, "xc_T": 2 * P}[what]
                    copy(softT[:, n % SOFT_TS, 0:size], B[:, 0:size]).then_inc(t_copied if what == "cP_T" else free, 1)
                elif what in ("O", "pool", "xP_O", "c_attn", "xc_attn"):
                    wait_full(act, job)
                    dst, src, _ = mixed(job, mix_hi)
                    copy(dst, src, gains[:, 5, i[0]:i[0] + 1] if what == "pool" else 1.0).then_inc(hi_ready, 1)
                if job == ("cS", 0):
                    own_keys(1)

            act.wait_ge(pad_ready, 1)
            nc.scalar.activation(cols[:, 5:6], cols[:, 4:5], ACT.Sqrt)
            act.wait_ge(gains_landed, 16)
            for i in range(4):
                if i < AHEAD:
                    split_hi(i)
                act.wait_ge(x_landed[i], 16)
                for k in range(CK * i, CK * i + CK):
                    copy(act_hi[:, k, :], xT[:, k, :], gains[:, GAIN["x"], k:k + 1]).then_inc(stream_hi, 1)
            for k in range(KT):
                square("x", k, xT[:, k, :], T)
                if k == 1:
                    for s in SPLITS_AT[0]:
                        split_hi(s)
            act.wait_ge(tables_landed, 16)
            for c in range(NC):
                if CHUNKS[c][4]:
                    take_out(c)
                if not halfway(c):
                    for s in SPLITS_AT.get(c + 1, ()):
                        split_hi(s)
                for job in JOBS[c]:
                    run(job)

        @block.vector
        def _(dve):
            V = nc.vector
            steps = [0]

            def then(instruction):
                steps[0] += 1
                instruction.then_inc(dve_step, 1)
                dve.wait_ge(dve_step, steps[0])

            def split_lo(c):
                dve.wait_ge(w_hi_ready, c + 1)
                V.tensor_tensor(lo_of(c), raw_of(c), hi_of(c).bitcast(F32), ALU.subtract).then_inc(w_lo_ready, 1)

            def less(out, src, scale, high):
                return V.scalar_tensor_tensor(out=out, in0=src, scalar=scale, in1=high.bitcast(F32), op0=ALU.mult, op1=ALU.subtract)

            def low_of_square(j):
                dve.wait_ge(hid_hi_ready, j + 1)
                V.tensor_tensor(hid_lo[:, j, :], hid[:, 1, j % 2, :], hid_hi[:, j, :].bitcast(F32), ALU.subtract).then_inc(hid_lo_ready, 1)

            def make_qblock(src, table):
                return V.tensor_tensor(qblock[:, :, :, :], src[:, :, SEQ:T].unsqueeze(3).broadcast_to([P, AT, DEC, 32]),
                                       table.unsqueeze(2).broadcast_to([P, AT, DEC, 32]), ALU.mult)

            def take_out(c):
                g, w, n, _, _ = CHUNKS[c]
                if w in ("ck", "cq", "up"):
                    dve.wait_ge(rstd_ready, {"ck": 2, "cq": 3, "up": 4}[w])
                if w == "cq" and n == 0:
                    wait_mixers_gone(dve)
                if w == "up" and n == 0:
                    wait_memory_stored(dve)
                if w == "ck" and n == 0:
                    dve.wait_ge(k_stored, 16)
                    dve.wait_ge(own_key_ready, DEC)
                    wait_full(dve, ("S", NH - 1))
                for x, bank in enumerate(banks_of(g)):
                    src = psum[:, bank, 0:T]
                    k = AT * n + x
                    free = bank_free[bank]
                    if x == 2 and halfway(c):
                        for s in SPLITS_AT.get(c + 1, ()):
                            split_lo(s)
                    if w != "cv":
                        wait_gemm(dve, g, x)
                    if w == "in" and n in (1, 2):
                        i = AT * g + x
                        if i == 0:
                            dve.wait_ge(rstd_ready, 1)
                            V.tensor_tensor(turned[:, 0, :], cos, rstd[:, 0, :], ALU.mult)
                            V.tensor_tensor(turned[:, 1, :], sin, rstd[:, 0, :], ALU.mult).then_inc(tables_ready, 1)
                            dve.wait_ge(tables_ready, 1)
                        dve.wait_ge(swapped_ready, i + 1)
                        if i >= 1:
                            dve.wait_ge(rope_done, i)
                        V.scalar_tensor_tensor(out=rope_a[:, i % 2, :], in0=src, scalar=HD ** -0.5 if n == 1 else 1.0, in1=turned[:, 0, :],
                                               op0=ALU.mult, op1=ALU.mult).then_inc(free, 1)
                        wait_gemm_out(dve, g, x)
                        dve.wait_ge(rope_b_ready, i + 1)
                        V.tensor_tensor((qT if n == 1 else kT)[:, x, :], rope_a[:, i % 2, :], rope_b[:, i % 2, :], ALU.add).then_inc(rope_done, 1)
                    elif w == "in":
                        dst = vT[:, x, :] if n == 3 else uext[:, x, STATE:STATE + T]
                        V.tensor_tensor(dst, src, rstd[:, 0, :], ALU.mult).then_inc(free, 1)
                    elif w == "ck":
                        V.tensor_tensor(mkT[:, k, :], psum[:, bank, 0:MEM], rstd[:, 1, 0:MEM], ALU.mult).then_inc(free, 1)
                    elif w in ("out", "co"):
                        V.tensor_tensor(xT[:, k, :], src, xT[:, k, :], ALU.add).then_inc(free, 1)
                        for low in (k - 1,) * (x > 0) + (k,) * (x == 3):
                            dve.wait_ge(stream_hi, STREAM[w] + low + 1)
                            less(act_lo[:, low, :], xT[:, low, :], gains[:, GAIN[w], low:low + 1], act_hi[:, low, :]).then_inc(stream_lo, 1)
                    elif w == "cq":
                        V.scalar_tensor_tensor(out=q2T[:, k, :], in0=src, scalar=MHD ** -0.5, in1=rstd[:, 0, :], op0=ALU.mult, op1=ALU.mult).then_inc(free, 1)
                    elif w == "up":
                        if k >= 2:
                            dve.wait_ge(square_ready, k - 1)
                        V.scalar_tensor_tensor(out=hid[:, 0, k % 2, :], in0=src, scalar=0.0, in1=rstd[:, 1, :], op0=ALU.max, op1=ALU.mult).then_inc(free, 1)
                        if k >= 1:
                            low_of_square(k - 1)
                        if k == FT - 1:
                            low_of_square(k)
                    elif w == "down":
                        V.tensor_tensor(xT[:, k, :], src, xT[:, k, :], ALU.add).then_inc(free, 1)
                if w == "in" and n == 2:
                    dve.wait_ge(const_landed, 16)
                    make_qblock(qT, head_q).then_inc(qblock_ready, 1)
                if w == "cq":
                    for x in range(4):
                        wait_gemm_out(dve, g, x)
                    if n == 0:
                        wait_full(dve, ("cS", 1))
                    else:
                        dve.wait_ge(keys_used, KEYS_USED["xS", 0, 1])
                    make_qblock(q2T[:, n * AT:(n + 1) * AT, :], head_x[:, n * AT:(n + 1) * AT, :]).then_inc(qblock_ready, 1)

            def pool_differences():
                dve.wait_ge(state_landed, 16)
                dve.wait_ge(sums_ready, 4)
                W = max(WINDOWS)
                for g, w in enumerate(WINDOWS):
                    d, u = difference(g), uext[:, g, STATE:]
                    V.tensor_tensor(d[:, 0:W], d[:, 0:W], inv_count[:, g, :], ALU.mult)
                    V.scalar_tensor_tensor(out=d[:, W:SEQ], in0=d[:, W:SEQ], scalar=1.0 / w, in1=u[:, W:SEQ],
                                           op0=ALU.mult, op1=ALU.subtract)
                    then(V.tensor_reduce(d[:, SEQ:T], stateT[:, g, :, STATE - (w - 1):STATE], AX_X, ALU.add))
                    then(V.tensor_tensor(d[:, SEQ:T], d[:, SEQ:T], u[:, SEQ:T], ALU.add))
                    V.tensor_tensor(d[:, 0:W], d[:, 0:W], u[:, 0:W], ALU.subtract)
                    V.scalar_tensor_tensor(out=d[:, SEQ:T], in0=d[:, SEQ:T], scalar=1.0 / w, in1=u[:, SEQ:T],
                                           op0=ALU.mult, op1=ALU.subtract).then_inc(d_ready, 1)

            def softmax_open(job):
                what, *i = job
                B, slot = bank_of(job), SOFT[job] % SOFTS
                wait_full(dve, job)
                prior = before(SOFT, job, SOFTS)
                if prior:
                    wait_full(dve, SOFT_END[prior])
                if what == "S":
                    V.tensor_tensor(soft[:, slot, 0:3 * P], B[:, 0:3 * P], causal, ALU.add).then_inc(bank_free[PLACE[job][0]], 1)
                    wait_out(dve, job)
                    V.tensor_reduce(stats[:, slot, 0:1], soft[:, slot, 0:P], AX_X, ALU.max, negate=True)
                    V.tensor_reduce(stats[:, slot, 1:2], soft[:, slot, P:3 * P], AX_X, ALU.max, negate=True).then_inc(max_ready, 1)
                elif what == "cS":
                    V.tensor_reduce(stats[:, slot, 0:1], B[:, 0:NKEY], AX_X, ALU.max, negate=True).then_inc(max_ready, 1)
                else:
                    V.tensor_reduce(stats[:, slot, 0:2], B.rearrange("p (x n) -> p x n", x=2), AX_X, ALU.max, negate=True).then_inc(max_ready, 1)

            def softmax_close(job):
                what, *i = job
                slot = SOFT[job] % SOFTS
                if what == "S":
                    dve.wait_ge(exp_ready, i[0] + 1)
                else:
                    wait_out(dve, job)
                n = 1 if what == "cS" else 2
                then(V.reciprocal(stats[:, slot, 4:4 + n], stats[:, slot, 2:2 + n]))
                parts = {"S": [(0, P), (P, 3 * P)], "cS": [(0, NKEY)]}.get(what, [(0, MEM), (MEM, 2 * MEM)])
                for x, (a, b) in enumerate(parts):
                    last = V.tensor_scalar(soft[:, slot, a:b], soft[:, slot, a:b], stats[:, slot, 4 + x:5 + x], None, ALU.mult)
                last.then_inc(soft_ready, 1)

            def run(job):
                what, *i = job
                if what == "m_tile":
                    k = i[0]
                    dve.wait_ge(stream_hi, STREAM["m"] + k + 1)
                    less(act_lo[:, k, 0:MEM], memory(k), gains[:, GAIN["m"], k:k + 1], act_hi[:, k, 0:MEM]).then_inc(stream_lo, 1)
                    return
                if what == "differences":
                    pool_differences()
                    return
                B = bank_of(job)
                free = bank_free[PLACE[job][0]]
                if what == "stat":
                    m = NORM[i[0]]
                    n = MEM if i[0] == "m" else T
                    wait_out(dve, job)
                    V.reciprocal(rstd[:, m % 2, 0:n], std[:, 0:n]).then_inc(rstd_ready, 1)
                elif what == "stat_col":
                    wait_out(dve, job)
                    V.reciprocal(cols[:, 2:4], cols[:, 0:2]).then_inc(cols_ready, 1)
                elif what == "cP_T":
                    b = i[0]
                    dve.wait_ge(t_copied, b + 1)
                    if b:
                        wait_full(dve, ("cO", b - 1))
                    V.tensor_tensor(ownp[:, :], B[0:DEC, PAST:PAST + P], con("own", DEC)[:, b * P:(b + 1) * P], ALU.mult).then_inc(free, 1)
                elif what in ("cO", "xc_O"):
                    wait_full(dve, job)
                    prior = before(OPART, job, 2)
                    if prior:
                        wait_full(dve, OPART_END[prior])
                    diag = con("diag_q") if what == "cO" else con("diag_x")[:, 2 * i[1]:2 * i[1] + 2]
                    heads = diag.shape[1]
                    V.tensor_tensor(opart[:, OPART[job] % 2, :].rearrange("p (h n) -> p h n", h=heads), B.rearrange("p (h n) -> p h n", h=heads),
                                    diag.unsqueeze(2).broadcast_to([P, heads, CN // heads]), ALU.mult).then_inc(free, 1)
                elif what in ("O", "xP_O", "c_attn", "xc_attn", "pool"):
                    dve.wait_ge(hi_ready, HI[job] + 1)
                    dst, src, high = mixed(job, mix_lo)
                    if what == "pool":
                        less(dst, src, gains[:, 5, i[0]:i[0] + 1], high).then_inc(free, 1)
                    else:
                        V.tensor_tensor(dst, src, high.bitcast(F32), ALU.subtract).then_inc(free, 1)
            dve.wait_ge(gains_landed, 16)
            for k in range(KT):
                if k % CK == 0 and k // CK < AHEAD:
                    split_lo(k // CK)
                dve.wait_ge(stream_hi, k + 1)
                less(act_lo[:, k, :], xT[:, k, :], gains[:, GAIN["x"], k:k + 1], act_hi[:, k, :]).then_inc(stream_lo, 1)
            for s in SPLITS_AT[0]:
                split_lo(s)
            dve.wait_ge(tables_landed, 16)
            for c in range(NC):
                if CHUNKS[c][4]:
                    take_out(c)
                if not halfway(c):
                    for s in SPLITS_AT.get(c + 1, ()):
                        split_lo(s)
                opened = []
                for job in JOBS[c]:
                    if job[0] == "xS" and job not in SOFT:
                        while opened:
                            softmax_close(opened.pop(0))
                        continue
                    if job in SOFT:
                        softmax_open(job)
                        opened.append(job)
                        if len(opened) == 2:
                            softmax_close(opened.pop(0))
                        continue
                    while opened:
                        softmax_close(opened.pop(0))
                    run(job)
                while opened:
                    softmax_close(opened.pop(0))
            dve.wait_ge(rstd_ready, 5)
            dve.wait_ge(y_gained, KT)
            for h in range(4):
                V.tensor_tensor(yT[:, 2 * h:2 * h + 2, :], yT[:, 2 * h:2 * h + 2, :], rstd[:, 0, :].unsqueeze(1).broadcast_to([P, 2, T]), ALU.mult).then_inc(y_ready, 1)

        @block.gpsimd
        def _(gp):
            def add_squares(norm):
                m = NORM[norm]
                n = MEM if norm == "m" else T
                for k in range(1, AT if norm == "y" else KT):
                    gp.wait_ge(sq_ready, KT * m + k + 1)
                    if k > 1:
                        gp.wait_ge(sq_added, (KT - 1) * m + k - 1)
                    nc.gpsimd.tensor_tensor(ssq[:, m % 2, 0:n], ssq[:, m % 2, 0:n], sq[:, k % SQ_SLOTS, 0:n], ALU.add).then_inc(sq_added, 1)

            nc.gpsimd.memset(cols[:, 4:5], 1.0).then_inc(pad_ready, 1)
            nc.gpsimd.memset(uext[:, :, 0:STATE], 0.0).then_inc(pad_ready, 1)
            add_squares("x")
            gp.wait_ge(tables_ready, 1)
            for i in range(2 * AT):
                gp.wait_ge(swapped_ready, i + 1)
                if i >= 2:
                    gp.wait_ge(rope_done, i - 1)
                nc.gpsimd.tensor_tensor(rope_b[:, i % 2, :], swapped[:, i % 2, :], turned[:, 1, :], ALU.mult).then_inc(rope_b_ready, 1)
            add_squares("m")
            gp.wait_ge(pad_ready, 2)
            for f in range(AT):
                wait_gemm_out(gp, group["in", 0], f)
            end_ = STATE + SEQ
            src, dst = uext, sum_a
            for g, w in enumerate(WINDOWS):
                half = w // 2
                if g:
                    gp.wait_ge(sums_ready, g)
                nc.gpsimd.tensor_tensor(dst[:, g:, w - 1:end_], src[:, g:, w - 1:end_], src[:, g:, w - 1 - half:end_ - half], ALU.add).then_inc(sums_ready, 1)
                src, dst = dst, (sum_b, sum_a)[g % 2]
            add_squares("c")
            add_squares("f")
            add_squares("y")


WEIGHTS = ("w_in", "w_out", "w_cq", "w_ck", "w_cv", "w_co", "w_up", "w_down")
DEVICE_OUTPUTS = {
    "y": (P, KT, T), "k": (P, AT, T), "u": (P, AT, STATE + DEC), "mk": (P, KT, MEM),
    "v_prompt": (1, 1, SEQ, NH, HD), "v_sample": (1, DEC, 1, NH, HD), "mem_v_prompt": (1, 1, MEM, MH, MHD), "pool_sample": (1, DEC, STATE, AW),
}


def features_first(a):
    return a.T.reshape(-1, P, a.shape[0]).transpose(1, 0, 2)


def rows_first(a):
    return a.transpose(2, 1, 0).reshape(a.shape[2], -1)


def lay_out(inputs):
    a = {k: np.asarray(v) for k, v in inputs.items()}
    out = {}
    for w in WEIGHTS:
        rows, columns = a[w].shape[1:]
        out[w] = a[w][0].reshape(rows // (CK * P), CK, P, columns // CN, CN).transpose(3, 0, 2, 1, 4)
    out["x"] = features_first(np.concatenate([a["x_prompt"][0], a["x_sample"][:, 0]]))
    out["mem"] = features_first(a["mem_prompt"][0]).reshape(P, 2, 4 * MEM)
    out["gains"] = np.concatenate([a[g].reshape(-1, P).T for g in ("g_mix", "g_cross", "g_mlp", "g_final", "g_mem", "s_pool", "s_pool")], axis=1)
    out["w_pool"] = a["w_pool"][0].transpose(1, 0, 2).reshape(P, AW)
    out["state"] = a["state_pool"][0].reshape(DEC, STATE, AT, P).transpose(3, 2, 0, 1)
    out["state_pool"] = a["state_pool"]
    pages = a["cache_k"].shape[1]
    out["cache_k"] = a["cache_k"][0].reshape(pages, PAGE, AT, P).transpose(0, 3, 2, 1)
    out["cache_v"] = a["cache_v"][0].reshape(pages, PAGE, AW)
    out["mem_k"] = a["cache_mem_k"][0].reshape(DEC, MEM, 2, AT, P).transpose(0, 2, 4, 3, 1)
    out["mem_v"] = a["cache_mem_v"][0].reshape(DEC, 2, P, 2, CN).transpose(0, 3, 2, 1, 4).reshape(DEC, 2, P, 2 * CN)
    out["page_table"] = a["page_table"].reshape(1, -1)
    out["tables"], out["constants"] = CONSTANTS[:, :TABLE_COLS], CONSTANTS[:, TABLE_COLS:]
    return {f"in_{k}": np.ascontiguousarray(v) for k, v in out.items()}


def kernel(**inputs):
    import concourse.bacc as bacc
    from concourse.bass_utils import run_bass_kernel_spmd

    nc = bacc.Bacc("TRN2", target_bir_lowering=False, num_devices=1)
    arrays = lay_out(inputs)
    ins = {name[3:]: nc.dram_tensor(name, a.shape, mybir.dt.from_np(a.dtype), kind="ExternalInput").ap() for name, a in arrays.items()}
    outs = {name: nc.dram_tensor(f"out_{name}", shape, F32, kind="ExternalOutput").ap() for name, shape in DEVICE_OUTPUTS.items()}
    build(nc, ins, outs)
    got = run_bass_kernel_spmd(nc, [arrays], core_ids=[0]).results[0]
    y, k, u = (rows_first(np.asarray(got[f"out_{name}"])) for name in ("y", "k", "u"))
    mk = rows_first(np.asarray(got["out_mk"]))
    pool_sample = np.concatenate([np.asarray(got["out_pool_sample"])[:, :, :STATE - 1], u[STATE:].reshape(1, DEC, 1, AW)], axis=2)
    return (y[:SEQ].reshape(1, SEQ, D), y[SEQ:].reshape(DEC, 1, D), k[:SEQ].reshape(1, 1, SEQ, NH, HD), got["out_v_prompt"],
            u[:STATE].reshape(1, 1, STATE, AW), mk.reshape(1, 1, MEM, MH, MHD), got["out_mem_v_prompt"],
            k[SEQ:].reshape(1, DEC, 1, NH, HD), got["out_v_sample"], pool_sample)
```
